# Optimizing a Trainium2 kernel written in Bass

```python
import jax, jax.numpy as jnp
from jax import lax
import numpy as np

D_MODEL = 1024
BATCH = 1
SEQ = 1024
DEPTH = 2

CTX_LEN = 256
GRID_W = 64
N_MIXERS = 3
EPS = 1e-6
CONV_WIDTH = 31
HEAD_DIM = 64
N_Q_HEADS = D_MODEL // HEAD_DIM
N_KV_HEADS = N_Q_HEADS // 4
Q_PER_KV = N_Q_HEADS // N_KV_HEADS
WINDOW = 128
ATTN_BLOCK = 128
ROPE_BASE = 10000.0
GMLP_CHUNK = 128
GMLP_WIDTH = 2 * D_MODEL
GMLP_GROUP_DIM = 128
GMLP_GROUPS = GMLP_WIDTH // GMLP_GROUP_DIM
FFN_DIM = 2816
FFN_CONV_WIDTH = 3

kernel_name = "hybrid_interleaved_conv_swa_gmlp_dit"

def rms_norm(x, g):
    xf = x.astype(jnp.float32)
    y = xf * lax.rsqrt(jnp.mean(xf * xf, axis=-1, keepdims=True) + EPS)
    return (y * g.astype(jnp.float32)).astype(x.dtype)

def layer_norm(x, g, b):
    xf = x.astype(jnp.float32)
    mu = jnp.mean(xf, axis=-1, keepdims=True)
    var = jnp.mean(jnp.square(xf - mu), axis=-1, keepdims=True)
    y = (xf - mu) * lax.rsqrt(var + EPS)
    return (y * g.astype(jnp.float32) + b.astype(jnp.float32)).astype(x.dtype)

def depthwise_conv(x, w, b):
    k = w.shape[0]
    half = (k - 1) // 2
    y = lax.conv_general_dilated(
        x, w[:, None, :].astype(x.dtype), window_strides=(1,), padding=[(half, half)],
        dimension_numbers=("NWC", "WIO", "NWC"), feature_group_count=x.shape[-1])
    return y + b

def axial_rope_tables(rows):
    row = jnp.repeat(jnp.arange(rows), GRID_W).astype(jnp.float32)
    col = jnp.tile(jnp.arange(GRID_W), rows).astype(jnp.float32)
    axis_dim = HEAD_DIM // 2
    inv_freq = ROPE_BASE ** (-jnp.arange(0, axis_dim, 2, dtype=jnp.float32) / axis_dim)
    ang_r = row[:, None] * inv_freq[None, :]
    ang_c = col[:, None] * inv_freq[None, :]
    ang = jnp.concatenate([ang_r, ang_r, ang_c, ang_c], axis=-1)
    return jnp.cos(ang), jnp.sin(ang)

def rotate_half(x):
    x1, x2 = jnp.split(x, 2, axis=-1)
    return jnp.concatenate([-x2, x1], axis=-1)

def apply_axial_rope(x, cos, sin):
    xr, xc = jnp.split(x, 2, axis=-1)
    rot = jnp.concatenate([rotate_half(xr), rotate_half(xc)], axis=-1)
    out = x * cos[None, :, None, :] + rot * sin[None, :, None, :]
    return out.astype(x.dtype)

def adaln_params(cond, w, b):
    mod = (jax.nn.silu(cond) @ w + b)[:, None, :]
    return jnp.split(mod, 6, axis=-1)

def conformer_conv(h, w_in, b_in, dw_w, dw_b, ln_g, ln_b, w_out, b_out):
    a, gt = jnp.split(h @ w_in + b_in, 2, axis=-1)
    z = a * jax.nn.sigmoid(gt)
    z = depthwise_conv(z, dw_w, dw_b)
    z = jax.nn.silu(layer_norm(z, ln_g, ln_b))
    return z @ w_out + b_out

def chunk_gmlp(h, w_in, b_in, ln_g, ln_b, w_s, b_s, w_out):
    bsz, length, _ = h.shape
    u, v = jnp.split(jax.nn.gelu(h @ w_in + b_in), 2, axis=-1)
    v = layer_norm(v, ln_g, ln_b)
    v = v.reshape(bsz, length // GMLP_CHUNK, GMLP_CHUNK, GMLP_GROUPS, GMLP_GROUP_DIM)
    s = jnp.einsum("gpq,bnqgc->bnpgc", w_s, v) + b_s.T[None, None, :, :, None]
    s = s.reshape(bsz, length, GMLP_WIDTH)
    return (u * s) @ w_out

def windowed_gqa(h, hc, w_qkv, sink, w_o, cos, sin, ctx_out):
    bsz, length, _ = h.shape
    n_ctx = hc.shape[1]
    nb = length // ATTN_BLOCK
    q_dim = N_Q_HEADS * HEAD_DIM
    kv_dim = N_KV_HEADS * HEAD_DIM
    scale = HEAD_DIM ** -0.5
    neg = jnp.float32(-1e30)

    q, k, v = jnp.split(h @ w_qkv, [q_dim, q_dim + kv_dim], axis=-1)
    q = apply_axial_rope(q.reshape(bsz, length, N_Q_HEADS, HEAD_DIM), cos, sin)
    k = apply_axial_rope(k.reshape(bsz, length, N_KV_HEADS, HEAD_DIM), cos, sin)
    v = v.reshape(bsz, length, N_KV_HEADS, HEAD_DIM)
    if ctx_out:
        qc, kc, vc = jnp.split(hc @ w_qkv, [q_dim, q_dim + kv_dim], axis=-1)
    else:
        kc, vc = jnp.split(hc @ w_qkv[:, q_dim:], 2, axis=-1)
    kc = kc.reshape(bsz, n_ctx, N_KV_HEADS, HEAD_DIM)
    vc = vc.reshape(bsz, n_ctx, N_KV_HEADS, HEAD_DIM)
    sink_f = sink.astype(jnp.float32).reshape(N_KV_HEADS, Q_PER_KV)

    pad = ((0, 0), (ATTN_BLOCK, ATTN_BLOCK), (0, 0), (0, 0))
    kp = jnp.pad(k, pad).reshape(bsz, nb + 2, ATTN_BLOCK, N_KV_HEADS, HEAD_DIM)
    vp = jnp.pad(v, pad).reshape(bsz, nb + 2, ATTN_BLOCK, N_KV_HEADS, HEAD_DIM)
    band = lambda t: jnp.concatenate([t[:, :-2], t[:, 1:-1], t[:, 2:]], axis=2)
    kw, vw = band(kp), band(vp)
    qb = q.reshape(bsz, nb, ATTN_BLOCK, N_KV_HEADS, Q_PER_KV, HEAD_DIM)

    s_win = jnp.einsum("bnqhgd,bnkhd->bnhgqk", qb, kw).astype(jnp.float32) * scale
    s_ctx = jnp.einsum("bnqhgd,bkhd->bnhgqk", qb, kc).astype(jnp.float32) * scale
    q_off = jnp.arange(ATTN_BLOCK)[:, None] + ATTN_BLOCK
    k_off = jnp.arange(3 * ATTN_BLOCK)[None, :]
    in_window = jnp.abs(q_off - k_off) <= WINDOW
    key_abs = (jnp.arange(nb)[:, None] - 1) * ATTN_BLOCK + jnp.arange(3 * ATTN_BLOCK)[None, :]
    valid = (key_abs >= 0) & (key_abs < length)
    mask = in_window[None] & valid[:, None, :]
    s_win = jnp.where(mask[None, :, None, None], s_win, neg)

    sk = sink_f[None, None, :, :, None, None]
    m = jnp.maximum(jnp.maximum(s_win.max(-1, keepdims=True), s_ctx.max(-1, keepdims=True)), sk)
    p_win = jnp.exp(s_win - m)
    p_ctx = jnp.exp(s_ctx - m)
    inv = 1.0 / (p_win.sum(-1, keepdims=True) + p_ctx.sum(-1, keepdims=True) + jnp.exp(sk - m))
    o = (jnp.einsum("bnhgqk,bnkhd->bnqhgd", p_win * inv, vw)
         + jnp.einsum("bnhgqk,bkhd->bnqhgd", p_ctx * inv, vc))
    y = o.astype(h.dtype).reshape(bsz, length, q_dim) @ w_o

    if not ctx_out:
        return y, None
    qc = qc.reshape(bsz, n_ctx, N_KV_HEADS, Q_PER_KV, HEAD_DIM)
    sc = jnp.einsum("bqhgd,bkhd->bhgqk", qc, kc).astype(jnp.float32) * scale
    skc = sink_f[None, :, :, None, None]
    mc = jnp.maximum(sc.max(-1, keepdims=True), skc)
    pc = jnp.exp(sc - mc)
    pc = pc / (pc.sum(-1, keepdims=True) + jnp.exp(skc - mc))
    oc = jnp.einsum("bhgqk,bkhd->bqhgd", pc, vc).astype(hc.dtype)
    yc = oc.reshape(bsz, n_ctx, q_dim) @ w_o
    return y, yc

def conv_ffn(h, w_up, conv_w, conv_b, w_down):
    z = depthwise_conv(h @ w_up, conv_w, conv_b)
    gate, val = jnp.split(z, 2, axis=-1)
    return (jax.nn.silu(gate) * val) @ w_down

def setup_inputs(seed: int = 0) -> dict:
    key = jax.random.key(seed)
    keys = jax.random.split(key, 32)
    ks = [keys[i] for i in range(32)]
    counter = [0]

    def nrm(shape, s):
        k = ks[counter[0]]
        counter[0] += 1
        return jax.random.normal(k, shape, jnp.float32) * s

    D = D_MODEL
    n_a = len(range(0, DEPTH, N_MIXERS))
    n_b = len(range(1, DEPTH, N_MIXERS))
    n_c = len(range(2, DEPTH, N_MIXERS))
    qkv_dim = (N_Q_HEADS + 2 * N_KV_HEADS) * HEAD_DIM
    return {
        "x": nrm((BATCH, SEQ, D), 1.0),
        "c": nrm((BATCH, D), 1.0),
        "ctx": nrm((BATCH, CTX_LEN, D), 1.0),
        "c_ctx": nrm((D,), 1.0),
        "ada_w": nrm((DEPTH, D, 6 * D), 0.5 * D ** -0.5),
        "ada_b": nrm((DEPTH, 6 * D), 0.02),
        "norm_g": 1.0 + nrm((DEPTH, 4, D), 0.02),
        "ffn_w_up": nrm((DEPTH, D, 2 * FFN_DIM), D ** -0.5),
        "ffn_conv_w": nrm((DEPTH, FFN_CONV_WIDTH, 2 * FFN_DIM), FFN_CONV_WIDTH ** -0.5),
        "ffn_conv_b": nrm((DEPTH, 2 * FFN_DIM), 0.02),
        "ffn_w_down": nrm((DEPTH, FFN_DIM, D), FFN_DIM ** -0.5),
        "cm_w_in": nrm((n_a, D, 2 * D), D ** -0.5),
        "cm_b_in": nrm((n_a, 2 * D), 0.02),
        "cm_dw_w": nrm((n_a, CONV_WIDTH, D), CONV_WIDTH ** -0.5),
        "cm_dw_b": nrm((n_a, D), 0.02),
        "cm_ln_g": 1.0 + nrm((n_a, D), 0.02),
        "cm_ln_b": nrm((n_a, D), 0.02),
        "cm_w_out": nrm((n_a, D, D), D ** -0.5),
        "cm_b_out": nrm((n_a, D), 0.02),
        "attn_w_qkv": nrm((n_b, D, qkv_dim), D ** -0.5),
        "attn_sink": nrm((n_b, N_Q_HEADS), 0.5),
        "attn_w_o": nrm((n_b, N_Q_HEADS * HEAD_DIM, D), D ** -0.5),
        "gm_w_in": nrm((n_c, D, 2 * GMLP_WIDTH), D ** -0.5),
        "gm_b_in": nrm((n_c, 2 * GMLP_WIDTH), 0.02),
        "gm_ln_g": 1.0 + nrm((n_c, GMLP_WIDTH), 0.02),
        "gm_ln_b": nrm((n_c, GMLP_WIDTH), 0.02),
        "gm_w_s": nrm((n_c, GMLP_GROUPS, GMLP_CHUNK, GMLP_CHUNK), GMLP_CHUNK ** -0.5),
        "gm_b_s": 1.0 + nrm((n_c, GMLP_GROUPS, GMLP_CHUNK), 0.02),
        "gm_w_out": nrm((n_c, GMLP_WIDTH, D), GMLP_WIDTH ** -0.5),
    }

def reference(x, c, ctx, c_ctx, ada_w, ada_b, norm_g, ffn_w_up, ffn_conv_w, ffn_conv_b, ffn_w_down,
              cm_w_in, cm_b_in, cm_dw_w, cm_dw_b, cm_ln_g, cm_ln_b, cm_w_out, cm_b_out,
              attn_w_qkv, attn_sink, attn_w_o,
              gm_w_in, gm_b_in, gm_ln_g, gm_ln_b, gm_w_s, gm_b_s, gm_w_out):
    length = x.shape[1]
    ROWS = length // GRID_W
    cos, sin = axial_rope_tables(ROWS)
    ctx_readers = [i for i in range(DEPTH) if i % N_MIXERS == 1]
    last_reader = max(ctx_readers) if ctx_readers else -1

    h, hc = x, ctx
    for i in range(DEPTH):
        kind, j = i % N_MIXERS, i // N_MIXERS
        use_ctx = i <= last_reader
        ctx_full = i < last_reader

        sh1, sc1, g1, sh2, sc2, g2 = adaln_params(c, ada_w[i], ada_b[i])
        a = rms_norm(h, norm_g[i, 0]) * (1.0 + sc1) + sh1
        if use_ctx:
            csh1, csc1, cg1, csh2, csc2, cg2 = adaln_params(c_ctx[None, :], ada_w[i], ada_b[i])
            ac = rms_norm(hc, norm_g[i, 0]) * (1.0 + csc1) + csh1

        if kind == 0:
            cm = (cm_w_in[j], cm_b_in[j], cm_dw_w[j], cm_dw_b[j], cm_ln_g[j], cm_ln_b[j], cm_w_out[j], cm_b_out[j])
            y = conformer_conv(a, *cm)
            yc = conformer_conv(ac, *cm) if ctx_full else None
        elif kind == 1:
            y, yc = windowed_gqa(a, ac, attn_w_qkv[j], attn_sink[j], attn_w_o[j], cos, sin, ctx_full)
        else:
            gm = (gm_w_in[j], gm_b_in[j], gm_ln_g[j], gm_ln_b[j], gm_w_s[j], gm_b_s[j], gm_w_out[j])
            y = chunk_gmlp(a, *gm)
            yc = chunk_gmlp(ac, *gm) if ctx_full else None

        h = h + g1 * rms_norm(y, norm_g[i, 1])
        f = conv_ffn(rms_norm(h, norm_g[i, 2]) * (1.0 + sc2) + sh2,
                     ffn_w_up[i], ffn_conv_w[i], ffn_conv_b[i], ffn_w_down[i])
        h = h + g2 * rms_norm(f, norm_g[i, 3])

        if ctx_full:
            hc = hc + cg1 * rms_norm(yc, norm_g[i, 1])
            fc = conv_ffn(rms_norm(hc, norm_g[i, 2]) * (1.0 + csc2) + csh2,
                          ffn_w_up[i], ffn_conv_w[i], ffn_conv_b[i], ffn_w_down[i])
            hc = hc + cg2 * rms_norm(fc, norm_g[i, 3])
    return h


_drawn_inputs = setup_inputs


def setup_inputs(seed=0):
    import zlib

    import numpy as np

    out = dict(_drawn_inputs(seed))
    spreads = {}
    factors = {'norm_g': 3.151,
     'ffn_conv_b': 5.347,
     'cm_b_in': 7.487,
     'cm_dw_b': 4.276,
     'cm_ln_g': 7.075,
     'cm_ln_b': 7.895,
     'cm_b_out': 4.562,
     'attn_sink': 64.0}
    for name, (base, spread) in spreads.items():
        noise = np.random.default_rng([zlib.crc32(name.encode()), seed]).standard_normal(out[name].shape)
        drawn = base * np.exp(spread * noise) if base else spread * noise
        out[name] = __import__('jax').numpy.asarray(drawn.astype(out[name].dtype))
    for name, factor in factors.items():
        out[name] = (out[name] * factor).astype(out[name].dtype)
    return out
```

```python
from contextlib import ExitStack

import numpy as np

import concourse.bass as bass
from concourse import mybir

ALU = mybir.AluOpType
ACT = mybir.ActivationFunctionType
F32 = mybir.dt.float32
F32R = mybir.dt.float32r
BF16 = mybir.dt.bfloat16
AX_X = mybir.AxisListType.X
ds = bass.ds

P = 128
D = 1024
KT = D // P
LAT, CTX = 1024, 256
TOK = LAT + CTX
FFN = 2816
FT = FFN // P
CW = 31
PAD = CW // 2
HD = 64
NQ, NKV = 16, 4
QPK = NQ // NKV
BLK = 128
NB = LAT // BLK
NEG = -1e30
EPS = 1e-6
GROUPS = [(0, 8), (8, 7), (15, 7)]
N_MOD = 48
ADA_FIRST = 8
ADA_PER = (3, 2)
assert ADA_FIRST + KT * sum(ADA_PER) == N_MOD
ZC = PAD + LAT + PAD + CTX + PAD
CC = LAT + PAD + CTX
LAG = 5

VEC = {}


def _vec_layout():
    at = 0
    for name, n in (("ada_b0", 48), ("ada_b1", 48), ("norm_g", 64), ("cmb_in", 16), ("dw_w", 8 * CW), ("dw_b", 8),
                    ("ln_g", 8), ("ln_b", 8), ("b_out", 8), ("cond", 16), ("sink", 16),
                    ("cw0", 4 * 2 * FT), ("cw1", 4 * 2 * FT)):
        VEC[name] = (at, n)
        at += n
    return at


NV = _vec_layout()


def stream_units():
    at, out = 0, {}
    for name, n in (("glu", 16), ("cm_out", 8), ("ffn0", 68), ("qkv", 12), ("w_o", 8), ("ffn1", 68)):
        out[name] = at
        at += n
    return out, at


UNIT_AT, N_UNITS = stream_units()


def plan():
    A, B = dict(t0=0, n=640), dict(t0=640, n=640)
    A1, B1, C1 = dict(t0=0, n=512), dict(t0=512, n=512), dict(t0=LAT, n=CTX)
    ph = [dict(kind="ada"), dict(kind="mod", layer=0, first=0, last=16, used=ADA_FIRST, ready=0)]
    for n, (c, t, mod) in enumerate(((A, "t4", dict(layer=0, first=16, last=48, used=ADA_FIRST + KT * ADA_PER[0], ready=2)),
                                     (B, "c_tail", dict(layer=1, first=0, last=48, used=N_MOD, ready=4)))):
        ph += [dict(kind="pre", layer=0, which=0, chunk=c, w=640, t=t),
               dict(kind="glu", chunk=c, units="glu", pairs=8, ada_per=ADA_PER[n], ada=ADA_FIRST + n * KT * ADA_PER[0]),
               dict(kind="mod", **mod)]
    for c in (A, B):
        ph += [dict(kind="ln", chunk=c), dict(kind="lin", units="cm_out", pairs=4, chunk=c, y="y3", after_glu=c is A),
               dict(kind="post", layer=0, which=0, chunk=c, y="y3", t="t3")]
    for c, w in ((A, 644), (B, 640)):
        ph += [dict(kind="pre", layer=0, which=1, chunk=c, w=w, t="t4"),
               dict(kind="ffn", layer=0, chunk=c, w=w, pairs=34, units="ffn0"),
               dict(kind="post", layer=0, which=1, chunk=c, y="y4", t="t4")]
    for c, n in ((C1, 2), (A1, 6), (B1, 6)):
        ph += [dict(kind="pre", layer=1, which=0, chunk=c, w=c["n"], t="o32"), dict(kind="qkv", chunk=c, units="qkv", pairs=n)]
    for m, c in enumerate((A1, B1)):
        ph += [dict(kind="attn", half=m, chunk=c), dict(kind="lin", units="w_o", pairs=4, chunk=c, y=("qA", "qB")[m], after_glu=False),
               dict(kind="post", layer=1, which=0, chunk=c, y=("qA", "qB")[m], t="o32")]
    for c, w in ((A1, 516), (B1, 512)):
        ph += [dict(kind="pre", layer=1, which=1, chunk=c, w=w, t="t4"),
               dict(kind="ffn", layer=1, chunk=c, w=w, pairs=34, units="ffn1"),
               dict(kind="post", layer=1, which=1, chunk=c, y="y4", t="t4", store=True)]
    steps = dict(pre=11, post=9, ln=17, attn=2)
    at = dict(q=0, s=0, p=0, d=0, a=0, g=0, r=0, k=0, v=0)
    released = [None, None]
    for x in ph:
        x.update(at)
        at["q"] += x.get("pairs", 0)
        at["s"] += steps.get(x["kind"], 0)
        if x["kind"] == "ffn":
            at["p"] += FT
            at["d"] += 2 * KT
        if x["kind"] == "attn":
            at["a"] += 1
        if x["kind"] == "glu":
            at["g"] += 8
        if x["kind"] == "qkv":
            x["list"] = []
            for n in range(2 * x["pairs"]):
                kind = "kvqqqq"[n // 2]
                latent = x["chunk"]["t0"] < LAT
                u = dict(kind=kind, tile=n % 2 if n < 4 else n - 4, roped=latent and kind != "v",
                         r=at["r"], k=at["k"], v=at["v"], free=released[n % 2])
                if u["roped"]:
                    at["r"] += 1
                    released[n % 2] = ("rope", 3 * at["r"])
                if kind == "k":
                    at["k"] += 1
                    if not u["roped"]:
                        released[n % 2] = ("k_lo", at["k"])
                if kind == "v":
                    at["v"] += 1
                    released[n % 2] = ("v_turned", at["v"])
                x["list"].append(u)
    return ph, at["q"]


def backbone(nc, xT, wstream, adastream, vec, consts, bconsts, rope, out):
    ph, n_pairs = plan()
    with ExitStack() as ctx:
        at = [(nc.sbuf_base + 31) // 32 * 32]

        def take(nbytes):
            a = at[0]
            at[0] += (nbytes + 31) // 32 * 32
            assert at[0] <= nc.sbuf_usable_end, at[0]
            return a

        def sb(name, shape, dt, offset):
            return nc.alloc_sbuf_tensor_at(name, shape, dt, offset=offset)

        h = sb("h", [P, KT, TOK], F32, take(KT * TOK * 4))
        rA, rZ, rY, rF, rW = (take(n) for n in (2 * KT * 644 * 4, KT * ZC * 4, KT * CC * 4, 4 * 2592, 6 * KT * P * 4))
        a_hi = sb("a_hi", [P, KT, 644], F32R, rA)
        a_lo = sb("a_lo", [P, KT, 644], F32R, rA + KT * 644 * 4)
        ada_first = sb("ada_first", [P, ADA_FIRST, KT, 2 * P], F32, rA)
        z = sb("z", [P, KT, ZC], F32, rZ)
        c = sb("c", [P, KT, CC], F32, rY)
        ada_slot = [[c[:, :, CC - 512:CC - 256], c[:, :, CC - 256:CC], z[:, :, 2 * PAD + LAT:2 * PAD + LAT + CTX]],
                    [z[:, :, 0:256], z[:, :, 256:512]]]
        assert 3 * PAD + 640 < 2 * PAD + LAT and CC - 512 >= 640 - PAD and 512 <= 640 - PAD
        z_hi = sb("z_hi", [P, 8, 640], F32R, rZ)
        z_lo = sb("z_lo", [P, 8, 640], F32R, rZ + 8 * 640 * 4)
        ug = sb("ug", [P, 648], F32, rF)
        uv = sb("uv", [P, 648], F32, rF + 2592)
        cg = sb("cg", [P, 640], F32, rF + 2 * 2592)
        cv = sb("cv", [P, 640], F32, rF + 2 * 2592 + 2560)
        dw_acc = sb("dw_acc", [P, 1280], F32, rF + 2 * 2592)
        raw = sb("raw", [P, 2, KT, P], F32, rW)
        w_hi = sb("w_hi", [P, 2, KT, P], F32R, rW + 2 * KT * P * 4)
        w_lo = sb("w_lo", [P, 2, KT, P], F32R, rW + 4 * KT * P * 4)
        qs_hi = sb("qs_hi", [P, NQ, BLK], F32R, rA)
        qs_lo = sb("qs_lo", [P, NQ, BLK], F32R, rA + 8192)
        prob = [sb(f"prob{j}", [P, QPK, 5 * BLK], F32, rA + 16384 + 10240 * j) for j in range(2)]
        o_hi = sb("o_hi", [P, KT, 512], F32R, rA)
        o_lo = sb("o_lo", [P, KT, 512], F32R, rA + 16384)
        o32 = sb("o32", [P, KT, 512], F32, rZ)
        rb = [sb(f"rb{j}", [P, 512], F32, rZ + 2048 * j) for j in range(2)]
        tb = [sb(f"tb{j}", [P, 512], F32, rZ + 4096 + 2048 * j) for j in range(2)]
        qh = [sb(f"q{'AB'[j]}", [P, KT, 512], F32, rZ + 16384 * (j + 1)) for j in range(2)]
        ks = sb("ks", [P, NKV, TOK], F32R, rZ + 49152)
        v_sb = sb("v_sb", [P, TOK // BLK, NKV * HD], F32, rZ + 49152 + 20480)
        assert rZ + 49152 + 20480 + 10240 <= rF
        rope_sb = sb("rope_sb", [P, 2, LAT], F32, rF)
        pT = sb("pT", [P, 5, QPK * BLK], F32, rF)
        wide = {"y3": sb("y3", [P, KT, 640], F32, rZ), "t3": sb("t3", [P, KT, 640], F32, rZ + KT * 640 * 4),
                "y4": sb("y4", [P, KT, 644], F32, rY), "t4": sb("t4", [P, KT, 644], F32, rY + KT * 644 * 4 - 0),
                "qA": qh[0], "qB": qh[1], "o32": o32}

        def wide_ap(name, w):
            return c[:, :, CC - 640:CC] if name == "c_tail" else wide[name][:, :, 0:w]

        rms = sb("rms", [P, 644], F32, take(644 * 4))
        vec_sb = sb("vec_sb", [P, NV], F32, take(NV * 4))
        cst = sb("cst", [P, 3, P], F32, take(3 * P * 4))
        bcst = sb("bcst", [P, 3, P], BF16, take(3 * P * 2))
        silu_c = sb("silu_c", [P, KT, 2], F32, take(64))
        mod = [sb(f"mod{l}", [P, 2, 48], F32, take(384)) for l in range(2)]
        u_edge = sb("u_edge", [P, 2 * FT], F32, take(8 * FT))
        eps_t = sb("eps_t", [P, 1], F32, take(4))
        soft = sb("soft", [P, 5, 2, QPK], F32, take(160))
        ones, ident, rot = (cst[:, i, :] for i in range(3))
        b_ident, mask_left, mask_right = (bcst[:, i, :] for i in range(3))

        PS = ctx.enter_context(nc.psum_tensor("PS", [P, 8, 512], F32))

        def sem(name):
            return ctx.enter_context(nc.semaphore(name))

        loaded = [sem(f"loaded{j}") for j in range(2)]
        hi_ready, lo_ready = sem("hi_ready"), sem("lo_ready")
        unit_done, evacuated = sem("unit_done"), sem("evacuated")
        ada_begun = [sem(f"ada_begun{j}") for j in range(4)]
        ada_loaded = [sem(f"ada_loaded{j}") for j in range(3)]
        ada_used, mod_ready, cond_ready = sem("ada_used"), sem("mod_ready"), sem("cond_ready")
        const_loaded, rope_loaded = sem("const_loaded"), sem("rope_loaded")
        h_loaded = [sem(f"h_loaded{n}") for n in range(2)]
        small_set, pad_set = sem("small_set"), sem("pad_set")
        norm_step = sem("norm_step")
        glu_done, dw_even, dw_odd = sem("glu_done"), sem("dw_even"), sem("dw_odd")
        gate_conv, val_conv = sem("gate_conv"), sem("val_conv")
        silu_done, prod_done = sem("silu_done"), sem("prod_done")
        zh_done, zl_done, y_added = sem("zh_done"), sem("zl_done"), sem("y_added")
        rot_done, rope_step = sem("rot_done"), sem("rope_step")
        k_hi, k_lo = sem("k_hi"), sem("k_lo")
        v_turned, v_stored = sem("v_turned"), sem("v_stored")
        qs_cut, qs_ready = sem("qs_cut"), sem("qs_ready")
        scored, max_ready, neg_max = sem("scored"), sem("max_ready"), sem("neg_max")
        exp_done, sink_shifted, sink_done = sem("exp_done"), sem("sink_shifted"), sem("sink_done")
        den_ready, inv_ready, prob_scaled = sem("den_ready"), sem("inv_ready"), sem("prob_scaled")
        turned, pT_ready, pv_done, o_stored = sem("turned"), sem("pT_ready"), sem("pv_done"), sem("o_stored")
        stored = sem("stored")

        def above_zero(value):
            return not isinstance(value, int) or value > 0

        def repeat(eng, n, body):
            body(0)
            if n > 1:
                with eng.Fori(1, n) as i:
                    body(i)

        def first_of(i):
            return isinstance(i, int) and i == 0

        def col(name, n):
            return vec_sb[:, ds(VEC[name][0] + n, 1)]

        def two(ap2, w):
            return ap2.rearrange("p (a b) -> p a b", a=2)

        def slot(j, w):
            return PS[:, 2 * j:2 * j + 2, 0:w // 2]

        def misc(w):
            return PS[:, 4:6, 0:w // 2]

        def segments(t0, w):
            out = []
            if t0 < LAT:
                out.append((0, min(w, LAT - t0), 0))
            if t0 + w > LAT:
                out.append((max(0, LAT - t0), min(w, t0 + w - LAT), 1))
            return out

        def c_parts(t0, w):
            return [(t0 + o + (PAD if cond else 0), o, n) for o, n, cond in segments(t0, w)]

        def wide_rms(ap, w):
            return ap.unsqueeze(1).to_broadcast([P, KT, w])

        def attn_keys(n):
            window = [b for b in (n - 1, n, n + 1) if 0 <= b < NB]
            masks = {2 + i: (mask_left if b < n else mask_right) for i, b in enumerate(window) if b != n}
            return [LAT // BLK, LAT // BLK + 1] + window, masks

        block = ctx.enter_context(nc.Block())

        @block.sync
        def _(sp):
            sp.dma_start(vec_sb[:], vec).then_inc(const_loaded, 16)
            sp.dma_start(cst[:], consts).then_inc(const_loaded, 16)
            sp.dma_start(bcst[:], bconsts).then_inc(const_loaded, 16)
            for j in range(4):
                n = ADA_FIRST // 4
                sp.dma_start(ada_first[:, n * j:n * j + n], adastream[n * j:n * j + n].rearrange("g p k n -> p g k n")).then_inc(ada_begun[j], 16)
            for x in ph:
                if "pairs" not in x:
                    continue
                first = UNIT_AT[x["units"]]

                def load(i, x=x, first=first):
                    q = x["q"] + i
                    for j in range(2):
                        if above_zero(2 * q + j - 1):
                            sp.wait_ge(lo_ready, 2 * q + j - 1)
                        sp.dma_start(raw[:, j], wstream[first + 2 * i + j]).then_inc(loaded[j], 16)
                repeat(sp, x["pairs"], load)

        @block.gpsimd
        def _(pool):
            nc.gpsimd.memset(eps_t[:], EPS).then_inc(small_set, 1)
            pool.wait_ge(ada_used, ADA_FIRST)
            for o in (0, PAD + LAT, 2 * PAD + LAT + CTX):
                last = nc.gpsimd.memset(z[:, :, o:o + PAD], 0.0)
            last.then_inc(pad_set, 1)
            for x in ph:
                if x["kind"] == "glu":
                    if x["chunk"]["t0"] == 0:
                        pool.wait_ge(norm_step, x["s"])
                    else:
                        pool.wait_ge(dw_even, 17 * 8)
                        pool.wait_ge(norm_step, x["s"])

                    def load(i, x=x, n=x["ada_per"], slots=ada_slot[x["chunk"]["t0"] > 0], first=x["chunk"]["t0"] == 0):
                        for r in range(n):
                            if not first_of(i):
                                pool.wait_ge(ada_used, x["ada"] + n * (i - 1) + r + 1)
                            pool.dma_start(slots[r], adastream[x["ada"] + n * i + r]).then_inc(ada_loaded[r], 16)
                    repeat(pool, 8, load)
                if x["kind"] != "attn":
                    continue
                for g in range(16):
                    G = 16 * x["a"] + g
                    w = len(attn_keys(4 * x["half"] + g // 4)[0]) * BLK
                    pool.wait_ge(inv_ready, G + 1)
                    for hh in range(QPK):
                        pr = prob[g % 2][:, hh, 0:w]
                        nc.gpsimd.tensor_scalar(pr, pr, soft[:, 4, g % 2, hh:hh + 1], 1.0, ALU.mult,
                                                ALU.mult).then_inc(prob_scaled, 1)

        @block.scalar
        def _(act):
            A = nc.scalar.activation

            def split(q, j):
                if isinstance(q, int) and q >= n_pairs:
                    return
                act.wait_ge(loaded[j], 16 * q + 16)
                if above_zero(2 * q + j - 1):
                    act.wait_ge(unit_done, 2 * q + j - 1)
                A(w_hi[:, j], raw[:, j], ACT.Copy).then_inc(hi_ready, 1)

            def squares(s, src, t):
                if above_zero(s):
                    act.wait_ge(norm_step, s)
                A(t, src, ACT.Square).then_inc(norm_step, 1)

            def root(s, w):
                act.wait_ge(norm_step, s)
                A(two(rms[:, 0:w], w), misc(w), ACT.Sqrt, bias=eps_t[:]).then_inc(norm_step, 1)

            for t0 in (0, 640):
                act.dma_start(h[:, :, t0:t0 + 640], xT[:, :, t0:t0 + 640]).then_inc(h_loaded[t0 > 0], 16)
            act.wait_ge(const_loaded, 48)
            act.wait_ge(small_set, 1)
            cond = vec_sb[:, VEC["cond"][0]:VEC["cond"][0] + 16].rearrange("p (k a) -> p k a", a=2)
            A(silu_c[:], cond, ACT.Silu).then_inc(cond_ready, 1)
            split(0, 0)
            split(0, 1)
            for x in ph:
                kind, q0, s, ch = x["kind"], x["q"], x["s"], x.get("chunk")
                if kind in ("pre", "post", "ln"):
                    t0, w = ch["t0"], x.get("w", ch["n"])
                if kind == "pre":
                    t, hs = wide_ap(x["t"], w), h[:, :, t0:t0 + w]
                    if x["layer"] == 0 and x["which"] == 0:
                        act.wait_ge(h_loaded[t0 > 0], 16)
                    if x["t"] == "c_tail":
                        act.wait_ge(ada_used, ADA_FIRST + KT * ADA_PER[0])
                    if x["t"] == "o32" and x["r"]:
                        act.wait_ge(rope_step, 3 * x["r"])
                    if above_zero(x["k"]):
                        act.wait_ge(k_lo, x["k"])
                    if above_zero(x["v"]):
                        act.wait_ge(v_stored, x["v"])
                    squares(s, hs, t)
                    root(s + 5, w)
                    act.wait_ge(norm_step, s + 8)
                    act.wait_ge(mod_ready, 2 if x["layer"] == 0 and x["which"] == 0 else 6)
                    if above_zero(2 * q0):
                        act.wait_ge(unit_done, 2 * q0)
                    for k in range(KT):
                        for o, n, cnd in segments(t0, w):
                            m = mod[x["layer"]][:, cnd, 24 * x["which"]:24 * x["which"] + 24]
                            last = A(a_hi[:, k, o:o + n], t[:, k, o:o + n], ACT.Identity,
                                     scale=m[:, 8 + k:9 + k], bias=m[:, k:k + 1])
                    last.then_inc(norm_step, 1)
                if kind == "post":
                    if x["y"] == "y4":
                        act.wait_ge(y_added, x["d"])
                    else:
                        act.wait_ge(evacuated, 2 * q0)
                    squares(s, wide_ap(x["y"], w), wide_ap(x["t"], w))
                    root(s + 5, w)
                    if x.get("store"):
                        act.wait_ge(norm_step, s + 9)
                        act.dma_start(out[:, :, t0:t0 + w], h[:, :, t0:t0 + w]).then_inc(stored, 16)
                if kind == "ln":
                    act.wait_ge(norm_step, s + 6)
                    for co, o, n in c_parts(t0, w):
                        last = A(wide["t3"][:, :, o:o + n], c[:, :, co:co + n], ACT.Square)
                    last.then_inc(norm_step, 1)
                    root(s + 11, w)
                    act.wait_ge(norm_step, s + 14)
                    for k in range(KT):
                        for co, o, n in c_parts(t0, w):
                            last = A(wide["t3"][:, k, o:o + n], c[:, k, co:co + n], ACT.Silu,
                                     scale=col("ln_g", k), bias=col("ln_b", k))
                    last.then_inc(norm_step, 1)
                    act.wait_ge(norm_step, s + 15)
                    act.wait_ge(unit_done, 2 * q0)
                    A(a_hi[:, :, 0:w], wide["t3"][:, :, 0:w], ACT.Copy).then_inc(norm_step, 1)
                if kind == "glu":
                    def body(i, x=x):
                        q, g = x["q"] + i, x["g"] + i
                        if above_zero(g):
                            act.wait_ge(glu_done, g)
                        act.wait_ge(unit_done, 2 * q + 1)
                        A(two(ug[:, 0:640], 640), slot(0, 640), ACT.Identity, bias=col("cmb_in", i)).then_inc(evacuated, 1)
                        split(q + 1, 0)
                        act.wait_ge(unit_done, 2 * q + 2)
                        A(two(uv[:, 0:640], 640), slot(1, 640), ACT.Sigmoid, bias=col("cmb_in", 8 + i)).then_inc(evacuated, 1)
                        split(q + 1, 1)
                    repeat(act, 8, body)
                if kind == "lin":
                    w = ch["n"]
                    y = wide[x["y"]]

                    def body(i, x=x, w=w, y=y):
                        q = x["q"] + i
                        for j in range(2):
                            if not (x["after_glu"] and first_of(i) and j == 0):
                                split(q + j, 1 - j)
                            act.wait_ge(unit_done, 2 * q + j + 1)
                            dst = y[:, ds(2 * i + j, 1), 0:w].rearrange("p o (a b) -> p (o a) b", a=2)
                            if x["units"] == "cm_out":
                                A(dst, slot(j, w), ACT.Identity, bias=col("b_out", 2 * i + j)).then_inc(evacuated, 1)
                            else:
                                A(dst, slot(j, w), ACT.Copy).then_inc(evacuated, 1)
                    if x["units"] == "w_o":
                        act.wait_ge(o_stored, 32 * x["a"])
                        act.wait_ge(norm_step, x["s"] - 2)
                        A(o_hi[:], o32[:], ACT.Copy).then_inc(norm_step, 1)
                        act.wait_ge(norm_step, x["s"])
                    repeat(act, 4, body)
                if kind == "ffn":
                    w, n_out = x["w"], ch["n"]
                    q, p, d = x["q"], x["p"], x["d"]
                    for gi, (f0, nf) in enumerate(GROUPS):
                        def zh(p, i):
                            act.wait_ge(prod_done, p + 1)
                            A(z_hi[:, ds(i, 1), 0:n_out], cv[:, 0:n_out].unsqueeze(1), ACT.Copy).then_inc(zh_done, 1)

                        def up(i, q=q, p=p, d=d):
                            q, p = q + i, p + i
                            split(q, 1)
                            if above_zero(3 * p):
                                act.wait_ge(gate_conv, 3 * p)
                            if first_of(i):
                                if above_zero(d):
                                    act.wait_ge(y_added, d)
                            act.wait_ge(unit_done, 2 * q + 1)
                            A(two(ug[:, 0:w], w), slot(0, w), ACT.Copy).then_inc(evacuated, 1)
                            if not first_of(i):
                                zh(p - 1, i - 1)
                            split(q + 1, 0)
                            if above_zero(3 * p):
                                act.wait_ge(val_conv, 3 * p)
                            act.wait_ge(unit_done, 2 * q + 2)
                            A(two(uv[:, 0:w], w), slot(1, w), ACT.Copy).then_inc(evacuated, 1)
                            act.wait_ge(gate_conv, 3 * p + 3)
                            A(cg[:, 0:n_out], cg[:, 0:n_out], ACT.Silu).then_inc(silu_done, 1)
                        repeat(act, nf, up)
                        q, p = q + nf, p + nf
                        zh(p - 1, nf - 1)

                        def down(i, q=q, p=p, d=d, gi=gi):
                            q = q + i
                            for j in range(2):
                                split(q + j, 1 - j)
                                act.wait_ge(unit_done, 2 * q + j + 1)
                                if gi == 0:
                                    dst = wide["y4"][:, ds(2 * i + j, 1), 0:n_out].rearrange("p o (a b) -> p (o a) b", a=2)
                                else:
                                    if above_zero(d + 2 * i + j - 1):
                                        act.wait_ge(y_added, d + 2 * i + j - 1)
                                    if first_of(i) and j == 0:
                                        act.wait_ge(zl_done, p)
                                    dst = two((ug, uv)[j][:, 0:n_out], n_out)
                                A(dst, slot(j, n_out), ACT.Copy).then_inc(evacuated, 1)
                        if q + 4 == n_pairs:
                            repeat(act, 3, down)
                            down(3)
                        else:
                            repeat(act, 4, down)
                        q += 4
                        if gi:
                            d += KT
                if kind == "qkv":
                    w, t0 = ch["n"], ch["t0"]
                    if t0 == LAT:
                        act.wait_ge(norm_step, s)
                        act.dma_start(rope_sb[:], rope).then_inc(rope_loaded, 16)
                    for i in range(x["pairs"]):
                        q = q0 + i
                        for j in range(2):
                            u = x["list"][2 * i + j]
                            split(q + j, 1 - j)
                            if u["free"] and u["free"][0] == "rope":
                                act.wait_ge(rope_step, u["free"][1])
                            if u["free"] and u["free"][0] == "k_lo":
                                act.wait_ge(k_lo, u["free"][1])
                            if u["free"] and u["free"][0] == "v_turned":
                                act.wait_ge(v_turned, u["free"][1])
                            if i == 0 and j == 0:
                                act.wait_ge(norm_step, s)
                            act.wait_ge(unit_done, 2 * q + j + 1)
                            A(two(rb[j][:, 0:w], w), slot(j, w), ACT.Copy).then_inc(evacuated, 1)
                        for j in range(2):
                            u = x["list"][2 * i + j]
                            g = 2 * u["tile"]
                            if u["kind"] == "k":
                                if u["roped"]:
                                    act.wait_ge(rope_step, 3 * u["r"] + 3)
                                else:
                                    act.wait_ge(evacuated, 2 * q + j + 1)
                                src = tb[j] if u["roped"] else rb[j]
                                A(ks[0:64, g, t0:t0 + w], src[0:64, 0:w], ACT.Copy)
                                A(ks[64:128, g + 1, t0:t0 + w], src[64:128, 0:w], ACT.Copy)
                                A(ks[0:64, g + 1, t0:t0 + w], src[64:128, 0:w], ACT.Copy).then_inc(k_hi, 1)
                            if u["kind"] == "v":
                                act.wait_ge(v_turned, u["v"] + 1)
                                A(v_sb[:, t0 // BLK:(t0 + w) // BLK, u["tile"] * P:(u["tile"] + 1) * P],
                                  PS[:, 6 + j, 0:w].rearrange("p (a b) -> p a b", b=P), ACT.Copy).then_inc(v_stored, 1)
                if kind == "attn":
                    a0, half = x["a"], x["half"]

                    def cut(g, part):
                        if above_zero(64 * a0 + 4 * (g - 3) if g > 3 else 0):
                            act.wait_ge(scored, 64 * a0 + 4 * (g - 3) if g > 3 else 0)
                        if g == 0 and part == 0:
                            act.wait_ge(norm_step, s)
                            act.wait_ge(rope_step, 3 * x["r"])
                            act.wait_ge(k_lo, x["k"])
                            act.wait_ge(unit_done, 2 * q0)
                        cb, kv = (g // 4) * BLK, g % 4
                        sh = part // 2 * 64
                        dh = sh if part % 2 == 0 else 64 - sh
                        A(qs_hi[dh:dh + 64, 4 * kv + part // 2:4 * kv + 4:2, :], qh[half][sh:sh + 64, 2 * kv:2 * kv + 2, cb:cb + BLK],
                          ACT.Copy, scale=HD ** -0.5).then_inc(qs_cut, 1)

                    for g in range(3):
                        for part in range(4):
                            cut(g, part)
                    for n in range(64 + LAG):
                        g, hh, m = n // QPK, n % QPK, n - LAG
                        if m >= 0:
                            nk = len(attn_keys(4 * half + m // 16)[0])
                            act.wait_ge(turned, 64 * a0 + m + 1)
                            if above_zero(32 * a0 + m // 2 - 1):
                                act.wait_ge(pv_done, 32 * a0 + m // 2 - 1)
                            if m == 0 and a0 == 0:
                                act.wait_ge(rope_step, 3 * x["r"])
                            A(pT[:, 0:nk, m % QPK * BLK:(m % QPK + 1) * BLK],
                              PS[:, 4:6, :].rearrange("p a b -> p (a b)")[:, 0:nk * BLK].rearrange("p (a b) -> p a b", b=BLK),
                              ACT.Copy).then_inc(pT_ready, 1)
                        if n < 64:
                            N = 64 * a0 + n
                            w = len(attn_keys(4 * half + g // 4)[0]) * BLK
                            act.wait_ge(neg_max, N + 1)
                            if above_zero(N - 7):
                                act.wait_ge(turned, N - 7)
                            A(prob[g % 2][:, hh, 0:w], PS[:, 2 * (hh % 2):2 * (hh % 2) + 2, :].rearrange("p a b -> p (a b)")[:, 0:w],
                              ACT.Exp, bias=soft[:, 1, g % 2, hh:hh + 1], accum_out=soft[:, 2, g % 2, hh:hh + 1]).then_inc(exp_done, 1)
                            if hh == QPK - 1:
                                act.wait_ge(sink_shifted, 16 * a0 + g + 1)
                                A(soft[:, 3, g % 2, :], soft[:, 3, g % 2, :], ACT.Exp).then_inc(sink_done, 1)
                            if g + 3 < 16:
                                cut(g + 3, hh)
            act.wait_ge(stored, 32)

        @block.vector
        def _(dve):
            TT, TS, STT = nc.vector.tensor_tensor, nc.vector.tensor_scalar, nc.vector.scalar_tensor_tensor

            def split(q, j):
                if isinstance(q, int) and q >= n_pairs:
                    return
                dve.wait_ge(hi_ready, 2 * q + j + 1)
                TT(w_lo[:, j], raw[:, j], w_hi[:, j].bitcast(F32), ALU.subtract).then_inc(lo_ready, 1)

            def sum_tiles(s, t):
                for i, n in enumerate((4, 2, 1)):
                    dve.wait_ge(norm_step, s + i)
                    TT(t[:, 0:n], t[:, 0:n], t[:, n:2 * n], ALU.add).then_inc(norm_step, 1)

            def invert(s, w):
                dve.wait_ge(norm_step, s)
                nc.vector.reciprocal(rms[:, 0:w], rms[:, 0:w]).then_inc(norm_step, 1)

            dve.wait_ge(const_loaded, 48)
            split(0, 0)
            split(0, 1)
            for x in ph:
                kind, q0, s, ch = x["kind"], x["q"], x["s"], x.get("chunk")
                if kind in ("pre", "post", "ln"):
                    t0, w = ch["t0"], x.get("w", ch["n"])
                if kind == "mod":
                    l, f0, f1, ready = x["layer"], x["first"], x["last"], x["ready"]
                    at_b, at_g = VEC[f"ada_b{l}"][0], VEC["norm_g"][0] + 32 * l
                    dve.wait_ge(ada_used, x["used"])
                    for cnd in range(2):
                        sums = PS[:, 6, 2 * (N_MOD * l + f0):2 * (N_MOD * l + f1)].rearrange("p (f a) -> p a f", a=2)[:, cnd, :]
                        last = TT(mod[l][:, cnd, f0:f1], sums, vec_sb[:, at_b + f0:at_b + f1], ALU.add)
                    last.then_inc(mod_ready, 1)
                    dve.wait_ge(mod_ready, ready + 1)
                    for cnd in range(2):
                        for which in range(2):
                            m = mod[l][:, cnd, 24 * which:24 * which + 24]
                            g = at_g + 16 * which
                            if f0 <= 24 * which + 8 < f1:
                                last = STT(m[:, 8:16], m[:, 8:16], 1.0, vec_sb[:, g:g + 8], ALU.add, ALU.mult)
                            if f0 <= 24 * which + 16 < f1:
                                last = TT(m[:, 16:24], m[:, 16:24], vec_sb[:, g + 8:g + 16], ALU.mult)
                    last.then_inc(mod_ready, 1)
                    dve.wait_ge(mod_ready, ready + 2)
                if kind == "pre":
                    t, hs = wide_ap(x["t"], w), h[:, :, t0:t0 + w]
                    sum_tiles(s + 1, t)
                    invert(s + 6, w)
                    dve.wait_ge(norm_step, s + 7)
                    TT(t, hs, wide_rms(rms[:, 0:w], w), ALU.mult).then_inc(norm_step, 1)
                    dve.wait_ge(norm_step, s + 9)
                    for k in range(KT):
                        for o, n, cnd in segments(t0, w):
                            m = mod[x["layer"]][:, cnd, 24 * x["which"]:24 * x["which"] + 24]
                            last = TS(t[:, k, o:o + n], t[:, k, o:o + n], m[:, 8 + k:9 + k], m[:, k:k + 1], ALU.mult, ALU.add)
                    last.then_inc(norm_step, 1)
                    dve.wait_ge(norm_step, s + 10)
                    TT(a_lo[:, :, 0:w], t, a_hi[:, :, 0:w].bitcast(F32), ALU.subtract).then_inc(norm_step, 1)
                if kind == "post":
                    y, t = wide_ap(x["y"], w), wide_ap(x["t"], w)
                    sum_tiles(s + 1, t)
                    invert(s + 6, w)
                    dve.wait_ge(norm_step, s + 7)
                    TT(y, y, wide_rms(rms[:, 0:w], w), ALU.mult).then_inc(norm_step, 1)
                    dve.wait_ge(norm_step, s + 8)
                    for k in range(KT):
                        for o, n, cnd in segments(t0, w):
                            hk = h[:, k, t0 + o:t0 + o + n]
                            gate = mod[x["layer"]][:, cnd, 24 * x["which"] + 16 + k:24 * x["which"] + 17 + k]
                            last = STT(hk, y[:, k, o:o + n], gate, hk, ALU.mult, ALU.add)
                    last.then_inc(norm_step, 1)
                if kind == "ln":
                    t3 = wide["t3"]
                    dve.wait_ge(dw_even, 17 * 16)
                    dve.wait_ge(norm_step, s)
                    for co, o, n in c_parts(t0, w):
                        last = TT(t3[:, 0:4, o:o + n], c[:, 0:4, co:co + n], c[:, 4:8, co:co + n], ALU.add)
                    last.then_inc(norm_step, 1)
                    for i, m in enumerate((2, 1)):
                        dve.wait_ge(norm_step, s + 1 + i)
                        TT(t3[:, 0:m, 0:w], t3[:, 0:m, 0:w], t3[:, m:2 * m, 0:w], ALU.add).then_inc(norm_step, 1)
                    dve.wait_ge(norm_step, s + 4)
                    nc.vector.tensor_copy(two(rms[:, 0:w], w), misc(w)).then_inc(norm_step, 1)
                    dve.wait_ge(norm_step, s + 5)
                    for co, o, n in c_parts(t0, w):
                        last = TT(c[:, :, co:co + n], c[:, :, co:co + n], wide_rms(rms[:, o:o + n], n), ALU.subtract)
                    last.then_inc(norm_step, 1)
                    sum_tiles(s + 7, t3[:, :, 0:w])
                    invert(s + 12, w)
                    dve.wait_ge(norm_step, s + 13)
                    for co, o, n in c_parts(t0, w):
                        last = TT(c[:, :, co:co + n], c[:, :, co:co + n], wide_rms(rms[:, o:o + n], n), ALU.mult)
                    last.then_inc(norm_step, 1)
                    dve.wait_ge(norm_step, s + 16)
                    TT(a_lo[:, :, 0:w], t3[:, :, 0:w], a_hi[:, :, 0:w].bitcast(F32), ALU.subtract).then_inc(norm_step, 1)
                if kind == "glu":
                    first = ch["t0"] == 0
                    o0 = 0 if first else 640 - PAD
                    m = 640 - PAD if first else CC - o0
                    parts = [(PAD, 0, 640)] if first else [(PAD + 640, 0, LAT - 640), (2 * PAD + LAT, LAT - 640, CTX)]

                    def body(i, x=x, parts=parts, o0=o0, m=m):
                        q, g = x["q"] + i, x["g"] + i
                        if first_of(i):
                            dve.wait_ge(pad_set, 1)
                        dve.wait_ge(evacuated, 2 * q + 2)
                        for zo, o, n in parts:
                            last = TT(z[:, ds(i, 1), zo:zo + n], ug[:, o:o + n].unsqueeze(1), uv[:, o:o + n].unsqueeze(1), ALU.mult)
                        last.then_inc(glu_done, 1)
                        split(q + 1, 0)
                        split(q + 1, 1)
                        dve.wait_ge(glu_done, g + 1)
                        even, odd = c[:, ds(i, 1), o0:o0 + m], dw_acc[:, 0:m].unsqueeze(1)
                        for k in range(CW):
                            src, tap = z[:, ds(i, 1), o0 + k:o0 + k + m], col("dw_w", i * CW + k)
                            if k == 0:
                                TS(even, src, tap, col("dw_b", i), ALU.mult, ALU.add).then_inc(dw_even, 1)
                            elif k == 1:
                                if above_zero(17 * g):
                                    dve.wait_ge(dw_even, 17 * g)
                                TS(odd, src, tap, 0.0, ALU.mult, ALU.add).then_inc(dw_odd, 1)
                            elif k % 2 == 0:
                                dve.wait_ge(dw_even, 17 * g + k // 2)
                                STT(even, src, tap, even, ALU.mult, ALU.add).then_inc(dw_even, 1)
                            else:
                                dve.wait_ge(dw_odd, 15 * g + k // 2)
                                STT(odd, src, tap, odd, ALU.mult, ALU.add).then_inc(dw_odd, 1)
                        dve.wait_ge(dw_even, 17 * g + 16)
                        dve.wait_ge(dw_odd, 15 * g + 15)
                        TT(even, even, odd, ALU.add).then_inc(dw_even, 1)
                    repeat(dve, 8, body)
                if kind == "lin":
                    def body(i, x=x):
                        q = x["q"] + i
                        if not (x["after_glu"] and first_of(i)):
                            split(q, 1)
                        split(q + 1, 0)
                    if x["units"] == "w_o":
                        dve.wait_ge(norm_step, x["s"] - 1)
                        TT(o_lo[:], o32[:], o_hi[:].bitcast(F32), ALU.subtract).then_inc(norm_step, 1)
                    repeat(dve, 4, body)
                if kind == "ffn":
                    n_out, l = ch["n"], x["layer"]
                    head = ch["t0"] == 0
                    cut_at = LAT - ch["t0"] if ch["t0"] < LAT < ch["t0"] + n_out else None
                    q, p, d = x["q"], x["p"], x["d"]
                    for gi, (f0, nf) in enumerate(GROUPS):
                        def zl(p, i):
                            dve.wait_ge(zh_done, p + 1)
                            TT(z_lo[:, ds(i, 1), 0:n_out], cv[:, 0:n_out].unsqueeze(1), z_hi[:, ds(i, 1), 0:n_out].bitcast(F32),
                               ALU.subtract).then_inc(zl_done, 1)

                        def conv3(u, dst, signal, p, f):
                            tap = [col(f"cw{l}", f * 4 + t) for t in range(4)]
                            edge = u_edge[:, ds(f, 1)]
                            TS(dst[:, 0:n_out], u[:, 0:n_out], tap[1], tap[3], ALU.mult, ALU.add).then_inc(signal, 1)
                            dve.wait_ge(signal, 3 * p + 1)
                            cuts = [(1, n_out)] if cut_at is None else [(1, cut_at), (cut_at + 1, n_out)]
                            if not head:
                                STT(dst[:, 0:1], edge, tap[0], dst[:, 0:1], ALU.mult, ALU.add)
                            for lo, hi in cuts:
                                last = STT(dst[:, lo:hi], u[:, lo - 1:hi - 1], tap[0], dst[:, lo:hi], ALU.mult, ALU.add)
                            last.then_inc(signal, 1)
                            dve.wait_ge(signal, 3 * p + 2)
                            if head:
                                nc.vector.tensor_copy(edge, u[:, n_out - 1:n_out])
                                cuts = [(0, n_out)]
                            else:
                                cuts = [(0, n_out - 1)] if cut_at is None else [(0, cut_at - 1), (cut_at, n_out - 1)]
                            for lo, hi in cuts:
                                last = STT(dst[:, lo:hi], u[:, lo + 1:hi + 1], tap[2], dst[:, lo:hi], ALU.mult, ALU.add)
                            last.then_inc(signal, 1)

                        def up(i, q=q, p=p, f0=f0):
                            q, p = q + i, p + i
                            split(q, 1)
                            if above_zero(p):
                                dve.wait_ge(prod_done, p)
                            dve.wait_ge(evacuated, 2 * q + 1)
                            conv3(ug, cg, gate_conv, p, f0 + i)
                            if not first_of(i):
                                zl(p - 1, i - 1)
                            split(q + 1, 0)
                            if above_zero(p):
                                dve.wait_ge(zl_done, p)
                            dve.wait_ge(evacuated, 2 * q + 2)
                            conv3(uv, cv, val_conv, p, f0 + i + FT)
                            dve.wait_ge(silu_done, p + 1)
                            dve.wait_ge(val_conv, 3 * p + 3)
                            TT(cv[:, 0:n_out], cg[:, 0:n_out], cv[:, 0:n_out], ALU.mult).then_inc(prod_done, 1)
                        repeat(dve, nf, up)
                        q, p = q + nf, p + nf
                        zl(p - 1, nf - 1)

                        def down(i, q=q, d=d, gi=gi):
                            q = q + i
                            for j in range(2):
                                split(q + j, 1 - j)
                                if gi:
                                    dve.wait_ge(evacuated, 2 * q + j + 1)
                                    if gi == 2:
                                        dve.wait_ge(y_added, d + 2 * i + j - 7)
                                    yk = wide["y4"][:, ds(2 * i + j, 1), 0:n_out]
                                    TT(yk, (ug, uv)[j][:, 0:n_out].unsqueeze(1), yk, ALU.add).then_inc(y_added, 1)
                        if q + 4 == n_pairs:
                            repeat(dve, 3, down)
                            down(3)
                        else:
                            repeat(dve, 4, down)
                        q += 4
                        if gi:
                            d += KT
                if kind == "qkv":
                    w, t0 = ch["n"], ch["t0"]
                    if t0 == 0:
                        dve.wait_ge(rope_loaded, 16)
                    for i in range(x["pairs"]):
                        q = q0 + i
                        for j in range(2):
                            split(q + j, 1 - j)
                        for j in range(2):
                            u = x["list"][2 * i + j]
                            g = 2 * u["tile"]
                            r3 = 3 * u["r"]
                            if u["roped"]:
                                dve.wait_ge(evacuated, 2 * q + j + 1)
                                dve.wait_ge(k_hi, u["k"])
                                dve.wait_ge(k_lo, u["k"])
                                if above_zero(r3):
                                    dve.wait_ge(rope_step, r3)
                                TT(tb[j][:, 0:w], rb[j][:, 0:w], rope_sb[:, 0, t0:t0 + w], ALU.mult).then_inc(rope_step, 1)
                                dve.wait_ge(rot_done, u["r"] + 1)
                                dve.wait_ge(rope_step, r3 + 1)
                                TT(rb[j][:, 0:w], PS[:, 4 + j, 0:w], rope_sb[:, 1, t0:t0 + w], ALU.mult).then_inc(rope_step, 1)
                                dve.wait_ge(rope_step, r3 + 2)
                                dst = tb[j][:, 0:w] if u["kind"] == "k" else qh[t0 // 512][:, u["tile"], 0:w]
                                TT(dst, tb[j][:, 0:w], rb[j][:, 0:w], ALU.add).then_inc(rope_step, 1)
                            if u["kind"] == "k":
                                dve.wait_ge(k_hi, u["k"] + 1)
                                src = tb[j] if u["roped"] else rb[j]
                                TT(ks[64:128, g, t0:t0 + w], src[0:64, 0:w], ks[0:64, g, t0:t0 + w].bitcast(F32), ALU.subtract)
                                TT(ks[64:128, g + 1, t0:t0 + w], src[64:128, 0:w], ks[64:128, g + 1, t0:t0 + w].bitcast(F32),
                                   ALU.subtract).then_inc(k_lo, 1)
                if kind == "attn":
                    a0, half = x["a"], x["half"]

                    def cut(g, part):
                        dve.wait_ge(qs_cut, 64 * a0 + 4 * g + part + 1)
                        cb, kv = (g // 4) * BLK, g % 4
                        sh = part // 2 * 64
                        dh = sh if part % 2 == 0 else 64 - sh
                        heads = slice(4 * kv + part // 2, 4 * kv + 4, 2)
                        STT(qs_lo[dh:dh + 64, heads, :], qh[half][sh:sh + 64, 2 * kv:2 * kv + 2, cb:cb + BLK], HD ** -0.5,
                            qs_hi[sh:sh + 64, heads, :].bitcast(F32), ALU.mult, ALU.subtract).then_inc(qs_ready, 1)

                    for g in range(3):
                        for part in range(4):
                            cut(g, part)
                    for n in range(64 + LAG + 3):
                        g, hh, H = n // QPK, n % QPK, (n - LAG - 4) // 2
                        if H >= 0 and (n - LAG) % 2 == 0:
                            tile, cb = H // 2 % 4 * 2 + H % 2, H // 8 * BLK
                            dve.wait_ge(pv_done, 32 * a0 + H + 1)
                            nc.vector.tensor_copy(o32[0:64, tile, cb:cb + BLK], PS[0:64, 6 + H % 2, 0:BLK])
                            nc.vector.tensor_copy(o32[64:128, tile, cb:cb + BLK], PS[0:64, 6 + H % 2, BLK:2 * BLK]).then_inc(o_stored, 1)
                        if n < 64:
                            N, G = 64 * a0 + n, 16 * a0 + g
                            w = len(attn_keys(4 * half + g // 4)[0]) * BLK
                            dve.wait_ge(scored, N + 1)
                            if above_zero(N - 7):
                                dve.wait_ge(neg_max, N - 7)
                            nc.vector.reduce_max(soft[:, 0, g % 2, hh:hh + 1],
                                                 PS[:, 2 * (hh % 2):2 * (hh % 2) + 2, :].rearrange("p a b -> p (a b)")[:, 0:w],
                                                 AX_X).then_inc(max_ready, 1)
                            dve.wait_ge(max_ready, N + 1)
                            if above_zero(N - 7):
                                dve.wait_ge(exp_done, N - 7)
                            if above_zero(G - 1):
                                dve.wait_ge(sink_shifted, G - 1)
                            TS(soft[:, 1, g % 2, hh:hh + 1], soft[:, 0, g % 2, hh:hh + 1], col("sink", 4 * (g % 4) + hh), -1.0,
                               ALU.max, ALU.mult).then_inc(neg_max, 1)
                            if hh == QPK - 1:
                                at_sink = VEC["sink"][0] + 4 * (g % 4)
                                dve.wait_ge(neg_max, N + 1)
                                if above_zero(G - 1):
                                    dve.wait_ge(den_ready, G - 1)
                                TT(soft[:, 3, g % 2, :], vec_sb[:, at_sink:at_sink + QPK], soft[:, 1, g % 2, :], ALU.add).then_inc(sink_shifted, 1)
                        if n % QPK == 0 and 0 < n <= 64:
                            G, b = 16 * a0 + g - 1, (g - 1) % 2
                            dve.wait_ge(sink_done, G + 1)
                            TT(soft[:, 2, b, :], soft[:, 2, b, :], soft[:, 3, b, :], ALU.add).then_inc(den_ready, 1)
                            dve.wait_ge(den_ready, G + 1)
                            if above_zero(4 * (G - 1)):
                                dve.wait_ge(prob_scaled, 4 * (G - 1))
                            nc.vector.reciprocal(soft[:, 4, b, :], soft[:, 2, b, :]).then_inc(inv_ready, 1)
                        if 0 < n <= 52:
                            cut((n - 1) // 4 + 3, (n - 1) % 4)

        @block.tensor
        def _(pe):
            MM = nc.tensor.matmul

            def unit(q, j, hi, lo, w, tiles, before_last=None):
                pe.wait_ge(lo_ready, 2 * q + j + 1)
                if above_zero(2 * q + j - 1):
                    pe.wait_ge(evacuated, 2 * q + j - 1)
                n = w // 2
                for k in range(tiles):
                    if k == tiles - 1 and before_last:
                        before_last()
                    for p_, (wt, mv) in enumerate(((w_hi, hi), (w_hi, lo), (w_lo, hi))):
                        for m in range(2):
                            last = MM(PS[:, 2 * j + m, 0:n], wt[:, j, k, :], mv[:, k, m * n:(m + 1) * n],
                                      start=(k == 0 and p_ == 0), stop=(k == tiles - 1 and p_ == 2))
                last.then_inc(unit_done, 1)

            def average(s, t0_ap, w):
                pe.wait_ge(norm_step, s)
                n = w // 2
                for m in range(2):
                    last = MM(PS[:, 4 + m, 0:n], ones, t0_ap[:, m * n:(m + 1) * n], start=True, stop=True)
                last.then_inc(norm_step, 1)

            def ada_pair(g, weights):
                for r in range(2):
                    for k in range(KT):
                        last = MM(PS[:, 6, ds(4 * g + 2 * r, 2)], weights[:, k, r * P:(r + 1) * P], silu_c[:, k, :],
                                  start=(k == 0), stop=(k == KT - 1))
                last.then_inc(ada_used, 1)

            pe.wait_ge(const_loaded, 48)
            pe.wait_ge(cond_ready, 1)
            for x in ph:
                kind, q0, s, ch = x["kind"], x["q"], x["s"], x.get("chunk")
                if kind in ("pre", "post", "ln"):
                    t0, w = ch["t0"], x.get("w", ch["n"])
                if kind == "ada":
                    for g in range(ADA_FIRST):
                        if g % 2 == 0:
                            pe.wait_ge(ada_begun[g // 2], 16)
                        ada_pair(g, ada_first[:, g])
                if kind in ("pre", "post"):
                    average(s + 4, wide_ap(x["t"], w)[:, 0], w)
                if kind == "ln":
                    average(s + 3, wide["t3"][:, 0], w)
                    average(s + 10, wide["t3"][:, 0], w)
                if kind == "glu":
                    pe.wait_ge(norm_step, s)
                    def body(i, x=x):
                        for j in range(2):
                            unit(x["q"] + i, j, a_hi, a_lo, 640, KT)
                        for r, slot_r in enumerate(ada_slot[x["chunk"]["t0"] > 0]):
                            before = KT if x["chunk"]["t0"] > 0 else 0
                            pe.wait_ge(ada_loaded[r], 16 * (i + 1 + before))
                            ada_pair(x["ada"] + x["ada_per"] * i + r, slot_r)
                    repeat(pe, 8, body)
                if kind == "lin":
                    pe.wait_ge(norm_step, s)
                    hi, lo = (a_hi, a_lo) if x["units"] == "cm_out" else (o_hi, o_lo)
                    def body(i, x=x, hi=hi, lo=lo, w=ch["n"]):
                        for j in range(2):
                            unit(x["q"] + i, j, hi, lo, w, KT)
                    repeat(pe, 4, body)
                if kind == "ffn":
                    pe.wait_ge(norm_step, s)
                    q, p = x["q"], x["p"]
                    for gi, (f0, nf) in enumerate(GROUPS):
                        def up(i, q=q, w=x["w"]):
                            for j in range(2):
                                unit(q + i, j, a_hi, a_lo, w, KT)
                        repeat(pe, nf, up)
                        q, p = q + nf, p + nf

                        def z_whole(p=p):
                            pe.wait_ge(zl_done, p)

                        def down(i, q=q, p=p, nf=nf, n=ch["n"]):
                            for j in range(2):
                                if first_of(i) and j == 0:
                                    pe.wait_ge(zl_done, p - 1)
                                unit(q + i, j, z_hi, z_lo, n, nf, z_whole if first_of(i) and j == 0 else None)
                        repeat(pe, 4, down)
                        q += 4
                if kind == "qkv":
                    w, t0 = ch["n"], ch["t0"]
                    pe.wait_ge(norm_step, s)
                    for i in range(x["pairs"]):
                        q = q0 + i
                        for j in range(2):
                            unit(q, j, a_hi, a_lo, w, KT)
                        for j in range(2):
                            u = x["list"][2 * i + j]
                            pe.wait_ge(evacuated, 2 * q + j + 1)
                            if u["roped"]:
                                if above_zero(3 * (u["r"] - 1)):
                                    pe.wait_ge(rope_step, 3 * (u["r"] - 1))
                                MM(PS[:, 4 + j, 0:w], rot, rb[j][:, 0:w], start=True, stop=True).then_inc(rot_done, 1)
                            if u["kind"] == "v":
                                if above_zero(u["v"] - 1):
                                    pe.wait_ge(v_stored, u["v"] - 1)
                                for b in range(w // BLK):
                                    last = nc.tensor.transpose(PS[:, 6 + j, b * BLK:(b + 1) * BLK], rb[j][:, b * BLK:(b + 1) * BLK], ident)
                                last.then_inc(v_turned, 1)
                if kind == "attn":
                    a0, half = x["a"], x["half"]

                    def scores(n):
                        g, hh, N = n // QPK, n % QPK, 64 * a0 + n
                        blk = 4 * half + g // 4
                        kv, head = g % 4, 4 * (g % 4) + hh
                        tiles, masks = attn_keys(blk)
                        wt = len(tiles)
                        pe.wait_ge(qs_ready, 64 * a0 + 4 * g + 4)
                        pe.wait_ge(k_lo, x["k"])
                        if above_zero(N - 1):
                            pe.wait_ge(exp_done, N - 1)
                        w0 = tiles[2] * BLK
                        pieces = [(0, 2, LAT), (2, 4, w0)] + [(4, 5, w0 + 2 * BLK)] * (wt == 5)
                        for c0, c1, src in pieces:
                            bank, o = 2 * (hh % 2) + c0 // 4, c0 % 4 * BLK
                            m = (c1 - c0) * BLK
                            masked = [c_ for c_ in range(c0, c1) if c_ in masks]
                            keys = ks[:, kv, src:src + m]
                            MM(PS[:, bank, o:o + m], qs_hi[:, head, :], keys, start=True, stop=False)
                            last = MM(PS[:, bank, o:o + m], qs_lo[:, head, :], keys, start=False, stop=not masked)
                            for c_ in masked:
                                mo = o + (c_ - c0) * BLK
                                last = MM(PS[:, bank, mo:mo + BLK], b_ident, masks[c_], start=False, stop=True)
                        last.then_inc(scored, 1)

                    def turn(m):
                        nk = len(attn_keys(4 * half + m // 16)[0])
                        pe.wait_ge(prob_scaled, 64 * a0 + m + 1)
                        if above_zero(64 * a0 + m):
                            pe.wait_ge(pT_ready, 64 * a0 + m)
                        for t in range(nk):
                            last = nc.tensor.transpose(PS[:, 4 + t // 4, t % 4 * BLK:(t % 4 + 1) * BLK],
                                                       prob[m // QPK % 2][:, m % QPK, t * BLK:(t + 1) * BLK], ident)
                        last.then_inc(turned, 1)

                    def values(H):
                        kv = H // 2 % 4
                        tiles, _ = attn_keys(4 * half + H // 8)
                        pe.wait_ge(pT_ready, 64 * a0 + 2 * H + 2)
                        pe.wait_ge(v_stored, x["v"])
                        if above_zero(32 * a0 + H - 1):
                            pe.wait_ge(o_stored, 32 * a0 + H - 1)
                        for t, tile in enumerate(tiles):
                            last = MM(PS[0:64, 6 + H % 2, 0:2 * BLK], v_sb[:, tile, kv * HD:(kv + 1) * HD],
                                      pT[:, t, H % 2 * 2 * BLK:(H % 2 + 1) * 2 * BLK], start=(t == 0), stop=(t == len(tiles) - 1))
                        last.then_inc(pv_done, 1)

                    scores(0)
                    for n in range(64 + LAG + 1):
                        if LAG <= n < 64 + LAG:
                            turn(n - LAG)
                        if n + 1 < 64:
                            scores(n + 1)
                        if n >= LAG + 2 and (n - LAG) % 2 == 0:
                            values((n - LAG - 2) // 2)


def shape_constants():
    consts = np.zeros((P, 3, P), np.float32)
    consts[:, 0] = 1.0 / D
    consts[:, 1] = np.eye(P)
    for m in range(P):
        if m % 32 < 16:
            consts[m + 16, 2, m] = -1.0
        else:
            consts[m - 16, 2, m] = 1.0
    i, j = np.arange(P)[:, None], np.arange(P)[None, :]
    b = np.zeros((P, 3, P), np.float32)
    b[:, 0] = np.eye(P)
    b[:, 1] = np.where(j < i, NEG, 0.0)
    b[:, 2] = np.where(j > i, NEG, 0.0)
    t = np.arange(LAT)
    inv = (np.float32(10000.0) ** (-np.arange(0, HD // 2, 2, dtype=np.float32) / np.float32(HD // 2))).astype(np.float32)
    row, colm = (t // 64).astype(np.float32), (t % 64).astype(np.float32)
    ar, ac = row[None, :] * inv[:, None], colm[None, :] * inv[:, None]
    ang = np.concatenate([ar, ar, ac, ac] * 2, axis=0).astype(np.float32)
    rope = np.stack([np.cos(ang), np.sin(ang)], axis=1).astype(np.float32)
    return consts, b, np.ascontiguousarray(rope)


def tiles_of(w, cols):
    k = w.shape[0] // P
    v = w.reshape(k, P, w.shape[1] // P, P)
    return [v[:, :, f, :].transpose(1, 0, 2) for f in cols]


def kernel(**inputs):
    import ml_dtypes
    import concourse.bacc as bacc
    from concourse.bass_utils import run_bass_kernel_spmd

    x = {k: np.asarray(v) for k, v in inputs.items()}

    def ffn_units(l):
        up, down = x["ffn_w_up"][l], x["ffn_w_down"][l]
        dv = down.reshape(FT, P, KT, P)
        units = []
        for f0, nf in GROUPS:
            for f in range(f0, f0 + nf):
                units += tiles_of(up, [f, FT + f])
            rows = list(range(f0, f0 + nf)) + [f0] * (8 - nf)
            units += [dv[rows][:, :, n, :].transpose(1, 0, 2) for n in range(KT)]
        return units

    units = tiles_of(x["cm_w_in"][0], [f for i in range(8) for f in (i, 8 + i)])
    units += tiles_of(x["cm_w_out"][0], range(8))
    units += ffn_units(0)
    units += tiles_of(x["attn_w_qkv"][0], [8, 9, 10, 11, 0, 1, 2, 3, 4, 5, 6, 7])
    units += tiles_of(x["attn_w_o"][0], range(8))
    units += ffn_units(1)
    wstream = np.stack(units)
    ada = [np.stack(tiles_of(x["ada_w"][l], range(N_MOD))).reshape(N_MOD // 2, 2, P, KT, P).transpose(0, 2, 3, 1, 4) for l in range(2)]
    adastream = np.concatenate(ada).reshape(N_MOD, P, KT, 2 * P)

    def cols(v):
        return np.ascontiguousarray(v.reshape(-1, P).T)

    def conv_cols(l):
        taps = np.stack([*x["ffn_conv_w"][l], x["ffn_conv_b"][l]])
        return taps.reshape(4, 2 * FT, P).transpose(2, 1, 0).reshape(P, -1)

    cond = np.stack([x["c"][0], x["c_ctx"]]).reshape(2, KT, P).transpose(2, 1, 0).reshape(P, 16)
    dw = x["cm_dw_w"][0].reshape(CW, KT, P).transpose(2, 1, 0).reshape(P, KT * CW)
    vec = np.concatenate([cols(x["ada_b"][0]), cols(x["ada_b"][1]), cols(x["norm_g"]), cols(x["cm_b_in"][0]), dw,
                          cols(x["cm_dw_b"][0]), cols(x["cm_ln_g"][0]), cols(x["cm_ln_b"][0]), cols(x["cm_b_out"][0]), cond,
                          np.broadcast_to(x["attn_sink"][0][None, :], (P, NQ)), conv_cols(0), conv_cols(1)], axis=1)
    xT = np.concatenate([x["x"][0], x["ctx"][0]]).T.reshape(KT, P, TOK).transpose(1, 0, 2)
    consts, masks, rope = shape_constants()
    arrays = {"xT": xT, "wstream": wstream, "adastream": adastream, "vec": vec, "consts": consts,
              "bconsts": masks.astype(ml_dtypes.bfloat16), "rope": rope}
    arrays = {k: np.ascontiguousarray(v) for k, v in arrays.items()}
    nc = bacc.Bacc("TRN2", target_bir_lowering=False, num_devices=1)
    args = [nc.dram_tensor(k, v.shape, mybir.dt.from_np(v.dtype), kind="ExternalInput").ap() for k, v in arrays.items()]
    out = nc.dram_tensor("out", (P, KT, LAT), F32, kind="ExternalOutput").ap()
    backbone(nc, *args, out)
    r = run_bass_kernel_spmd(nc, [arrays], core_ids=[0])
    o = r.results[0]["out"]
    return np.ascontiguousarray(o.transpose(2, 1, 0).reshape(1, LAT, D))
```

```python
from contextlib import ExitStack

import numpy as np

import concourse.bass as bass
from concourse import mybir

ALU = mybir.AluOpType
ACT = mybir.ActivationFunctionType
F32 = mybir.dt.float32
F32R = mybir.dt.float32r
BF16 = mybir.dt.bfloat16
AX_X = mybir.AxisListType.X
ds = bass.ds

P = 128
D = 1024
KT = D // P
LAT, CTX = 1024, 256
TOK = LAT + CTX
FFN = 2816
FT = FFN // P
CW = 31
PAD = CW // 2
N_EVEN, N_ODD = CW // 2 + 2, CW // 2
HD = 64
NQ, NKV = 16, 4
QPK = NQ // NKV
BLK = 128
NB = LAT // BLK
NEG = -1e30
EPS = 1e-6
GROUPS = [(0, 8), (8, 7), (15, 7)]
N_MOD = 48
ADA_FIRST = 8
ADA_PER = (3, 2)
assert ADA_FIRST + KT * sum(ADA_PER) == N_MOD
ZC = PAD + LAT + PAD + CTX + PAD
CC = LAT + PAD + CTX
LAG = 5

VEC = {}


def _vec_layout():
    at = 0
    for name, n in (("ada_b0", 48), ("ada_b1", 48), ("norm_g", 64), ("cmb_in", 16), ("dw_w", 8 * CW), ("dw_b", 8),
                    ("ln_g", 8), ("ln_b", 8), ("b_out", 8), ("cond", 16), ("sink", 16),
                    ("cw0", 4 * 2 * FT), ("cw1", 4 * 2 * FT)):
        VEC[name] = (at, n)
        at += n
    return at


NV = _vec_layout()


def stream_units():
    at, out = 0, {}
    for name, n in (("glu", 16), ("cm_out", 8), ("ffn0", 68), ("qkv", 12), ("w_o", 8), ("ffn1", 68)):
        out[name] = at
        at += n
    return out, at


UNIT_AT, N_UNITS = stream_units()


def plan():
    A, B = dict(t0=0, n=640), dict(t0=640, n=640)
    A1, B1, C1 = dict(t0=0, n=512), dict(t0=512, n=512), dict(t0=LAT, n=CTX)
    ph = []
    for n, (c, t, mod) in enumerate(((A, "t4", dict(layer=0, first=16, last=48, used=ADA_FIRST + KT * ADA_PER[0], ready=2)),
                                     (B, "c_tail", dict(layer=1, first=0, last=48, used=N_MOD, ready=4)))):
        ph += [dict(kind="pre", layer=0, which=0, chunk=c, w=640, t=t)]
        if c is A:
            ph[0]["mod"] = dict(layer=0, first=0, last=16, used=ADA_FIRST, ready=0)
            ph += [dict(kind="ada")]
        ph += [dict(kind="glu", chunk=c, units="glu", pairs=8, ada_per=ADA_PER[n], ada=ADA_FIRST + n * KT * ADA_PER[0]),
               dict(kind="mod", **mod)]
    ln_b = dict(kind="ln", chunk=B, stats_hosted=True)
    post_a = dict(kind="post", layer=0, which=0, chunk=A, y="y3", t="t3", hosted=True)
    ph += [dict(kind="ln", chunk=A), dict(kind="lin", units="cm_out", pairs=4, chunk=A, y="y3", after_glu=True, stats=ln_b),
           ln_b, post_a, dict(kind="lin", units="cm_out", pairs=4, chunk=B, y="c_head", after_glu=False, head=post_a),
           dict(kind="post", layer=0, which=0, chunk=B, y="c_head", t="t3")]
    pre_b = dict(kind="pre", layer=0, which=1, chunk=B, w=640, t="t4", hosted=True)
    post_a = dict(kind="post", layer=0, which=1, chunk=A, y="y4", t="t4", hosted=True)
    pre_a1 = dict(kind="pre", layer=1, which=0, chunk=A1, w=512, t="t4", hosted=True)
    post_b = dict(kind="post", layer=0, which=1, chunk=B, y="y4", t="t4", hosted=True)
    ph += [dict(kind="pre", layer=0, which=1, chunk=A, w=644, t="t4"),
           dict(kind="ffn", layer=0, chunk=A, w=644, pairs=34, units="ffn0", tail=pre_b), pre_b, post_a,
           dict(kind="ffn", layer=0, chunk=B, w=640, pairs=34, units="ffn0", head=post_a, tail=pre_a1), pre_a1,
           post_b, dict(kind="qkv", chunk=A1, units="qkv", pairs=6, order=[2, 3, 4, 5, 0, 1], head=post_b)]
    for c, n in ((C1, 2), (B1, 6)):
        ph += [dict(kind="pre", layer=1, which=0, chunk=c, w=c["n"], t="o32"),
               dict(kind="qkv", chunk=c, units="qkv", pairs=n, order=list(range(n)))]
    post_a = dict(kind="post", layer=1, which=0, chunk=A1, y="yA", t="qB", hosted=True)
    ph += [dict(kind="attn", half=0, chunk=A1), dict(kind="attn", half=1, chunk=B1),
           dict(kind="lin", units="w_o", pairs=4, chunk=A1, y="yA", half=0, after_glu=False), post_a,
           dict(kind="lin", units="w_o", pairs=4, chunk=B1, y="o32", half=1, after_glu=False, head=post_a),
           dict(kind="post", layer=1, which=0, chunk=B1, y="o32", t="qB")]
    pre_b = dict(kind="pre", layer=1, which=1, chunk=B1, w=512, t="t4", hosted=True)
    post_a = dict(kind="post", layer=1, which=1, chunk=A1, y="y4", t="t4", store=True, hosted=True)
    ph += [dict(kind="pre", layer=1, which=1, chunk=A1, w=516, t="t4"),
           dict(kind="ffn", layer=1, chunk=A1, w=516, pairs=34, units="ffn1", tail=pre_b), pre_b, post_a,
           dict(kind="ffn", layer=1, chunk=B1, w=512, pairs=34, units="ffn1", head=post_a),
           dict(kind="post", layer=1, which=1, chunk=B1, y="y4", t="t4", store=True)]
    steps = dict(pre=7, post=9, ln=13)
    at = dict(q=0, s=0, n=0, p=0, d=0, a=0, g=0, r=0, k=0, v=0)
    released = [None, None]
    for x in ph:
        x.update(at)
        at["q"] += x.get("pairs", 0)
        at["s"] += steps.get(x["kind"], 0)
        at["n"] += x["kind"] in ("pre", "ln")
        if x["kind"] == "ffn":
            at["p"] += FT
            at["d"] += 2 * KT
        if x["kind"] == "attn":
            at["a"] += 1
        if x["kind"] == "glu":
            at["g"] += 8
        if x["kind"] == "qkv":
            x["list"] = []
            for n in range(2 * x["pairs"]):
                at_unit = 2 * x["order"][n // 2] + n % 2
                kind = "kvqqqq"[at_unit // 2]
                latent = x["chunk"]["t0"] < LAT
                u = dict(kind=kind, tile=at_unit % 2 if at_unit < 4 else at_unit - 4, roped=latent and kind != "v",
                         r=at["r"], k=at["k"], v=at["v"], free=released[n % 2])
                if u["roped"]:
                    at["r"] += 1
                    released[n % 2] = ("rope", 3 * at["r"])
                if kind == "k":
                    at["k"] += 1
                    if not u["roped"]:
                        released[n % 2] = ("k_lo", at["k"])
                if kind == "v":
                    at["v"] += 1
                    released[n % 2] = ("v_turned", at["v"])
                x["list"].append(u)
    return ph, at["q"]


def backbone(nc, xT, wstream, adastream, vec, consts, bconsts, rope, out):
    ph, n_pairs = plan()
    with ExitStack() as ctx:
        at = [(nc.sbuf_base + 31) // 32 * 32]

        def take(nbytes):
            a = at[0]
            at[0] += (nbytes + 31) // 32 * 32
            assert at[0] <= nc.sbuf_usable_end, at[0]
            return a

        def sb(name, shape, dt, offset):
            return nc.alloc_sbuf_tensor_at(name, shape, dt, offset=offset)

        h = sb("h", [P, KT, TOK], F32, take(KT * TOK * 4))
        rA, rZ, rY, rF, rW = (take(n) for n in (2 * KT * 644 * 4, KT * ZC * 4, KT * CC * 4, 4 * 2592, 6 * KT * P * 4))
        a_hi = sb("a_hi", [P, KT, 644], F32R, rA)
        a_lo = sb("a_lo", [P, KT, 644], F32R, rA + KT * 644 * 4)
        ada_first = sb("ada_first", [P, ADA_FIRST, KT, 2 * P], F32, rA)
        z = sb("z", [P, KT, ZC], F32, rZ)
        c = sb("c", [P, KT, CC], F32, rY)
        ada_slot = [[c[:, :, CC - 512:CC - 256], c[:, :, CC - 256:CC], z[:, :, 2 * PAD + LAT:2 * PAD + LAT + CTX]],
                    [z[:, :, 0:256], z[:, :, 256:512]]]
        assert 3 * PAD + 640 < 2 * PAD + LAT and CC - 512 >= 640 - PAD and 512 <= 640 - PAD
        z_hi = sb("z_hi", [P, 8, 640], F32R, rZ)
        z_lo = sb("z_lo", [P, 8, 640], F32R, rZ + 8 * 640 * 4)
        ug = sb("ug", [P, 648], F32, rF)
        uv = sb("uv", [P, 648], F32, rF + 2592)
        cg = sb("cg", [P, 640], F32, rF + 2 * 2592)
        cv = sb("cv", [P, 640], F32, rF + 2 * 2592 + 2560)
        dw_acc = sb("dw_acc", [P, CC - 640 + PAD], F32, rF + 2 * 2592)
        ada_row = sb("ada_row", [2, 2, 2 * P], F32, rF + 2 * 2592 + 2688)
        assert (CC - 640 + PAD) * 4 <= 2688 and 2 * 2592 + 2688 + 2048 <= 4 * 2592
        raw = sb("raw", [P, 2, KT, P], F32, rW)
        w_hi = sb("w_hi", [P, 2, KT, P], F32R, rW + 2 * KT * P * 4)
        w_lo = sb("w_lo", [P, 2, KT, P], F32R, rW + 4 * KT * P * 4)
        qs_hi = sb("qs_hi", [P, NQ, BLK], F32R, rA)
        qs_lo = sb("qs_lo", [P, NQ, BLK], F32R, rA + 8192)
        prob = [sb(f"prob{j}", [P, QPK, 5 * BLK], F32, rA + 16384 + 10240 * j) for j in range(2)]
        o_hi = sb("o_hi", [P, KT, 512], F32R, rA)
        o_lo = sb("o_lo", [P, KT, 512], F32R, rA + 16384)
        o32 = sb("o32", [P, KT, 512], F32, rZ)
        rb = [sb(f"rb{j}", [P, 512], F32, rZ + 2048 * j) for j in range(2)]
        tb = [sb(f"tb{j}", [P, 512], F32, rZ + 4096 + 2048 * j) for j in range(2)]
        qh = [sb(f"q{'AB'[j]}", [P, KT, 512], F32, rZ + 16384 * (j + 1)) for j in range(2)]
        o_out = [o32, qh[0]]
        ks = sb("ks", [P, NKV, TOK], F32R, rZ + 49152)
        v_sb = sb("v_sb", [P, TOK // BLK, NKV * HD], F32, rZ + 49152 + 20480)
        assert rZ + 49152 + 20480 + 10240 <= rF
        rope_sb = sb("rope_sb", [P, 2, LAT], F32, rF)
        pT = sb("pT", [P, 5, QPK * BLK], F32, rF)
        wide = {"y3": sb("y3", [P, KT, 640], F32, rZ), "t3": sb("t3", [P, KT, 640], F32, rZ + KT * 640 * 4),
                "y4": sb("y4", [P, KT, 644], F32, rY), "t4": sb("t4", [P, KT, 644], F32, rY + KT * 644 * 4),
                "yA": sb("yA", [P, KT, 512], F32, rZ + 49152), "qB": qh[1], "o32": o32}

        def wide_ap(name, w):
            if name[:2] == "c_":
                return c[:, :, CC - 640:CC] if name == "c_tail" else c[:, :, 0:w]
            return wide[name][:, :, 0:w]

        rms = sb("rms", [P, 644], F32, take(644 * 4))
        vec_sb = sb("vec_sb", [P, NV], F32, take(NV * 4))
        cst = sb("cst", [P, 3, P], F32, take(3 * P * 4))
        bcst = sb("bcst", [P, 3, P], BF16, take(3 * P * 2))
        silu_c = sb("silu_c", [P, KT, 2], F32, take(64))
        mod = [sb(f"mod{l}", [P, 2, 48], F32, take(384)) for l in range(2)]
        u_edge = sb("u_edge", [P, 2 * FT], F32, take(8 * FT))
        eps_t = sb("eps_t", [P, 1], F32, take(4))
        soft = sb("soft", [P, 5, 2, QPK], F32, take(160))
        ones, ident, rot = (cst[:, i, :] for i in range(3))
        b_ident, mask_left, mask_right = (bcst[:, i, :] for i in range(3))

        PS = ctx.enter_context(nc.psum_tensor("PS", [P, 8, 512], F32))

        def sem(name):
            return ctx.enter_context(nc.semaphore(name))

        loaded = [sem(f"loaded{j}") for j in range(2)]
        hi_ready, lo_ready = sem("hi_ready"), sem("lo_ready")
        unit_done, evacuated = sem("unit_done"), sem("evacuated")
        ada_begun = [sem(f"ada_begun{j}") for j in range(4)]
        ada_loaded = [sem(f"ada_loaded{j}") for j in range(3)]
        ada_used, mod_ready, cond_ready = sem("ada_used"), sem("mod_ready"), sem("cond_ready")
        row_ready, ada_turned = sem("row_ready"), sem("ada_turned")
        const_loaded, rope_loaded = sem("const_loaded"), sem("rope_loaded")
        h_loaded = [sem(f"h_loaded{n}") for n in range(2)]
        eps_set, pad_set = sem("eps_set"), sem("pad_set")
        norm_step = sem("norm_step")
        in_normed, in_modulated, in_hi, in_lo = sem("in_normed"), sem("in_modulated"), sem("in_hi"), sem("in_lo")
        glu_done, dw_even, dw_odd = sem("glu_done"), sem("dw_even"), sem("dw_odd")
        gate_conv, val_conv = sem("gate_conv"), sem("val_conv")
        silu_done, prod_done = sem("silu_done"), sem("prod_done")
        zh_done, zl_done, y_added = sem("zh_done"), sem("zl_done"), sem("y_added")
        rot_done, rope_step = sem("rot_done"), sem("rope_step")
        k_hi, k_lo = sem("k_hi"), sem("k_lo")
        v_turned, v_stored = sem("v_turned"), sem("v_stored")
        qs_cut, qs_ready = sem("qs_cut"), sem("qs_ready")
        scored, max_ready, neg_max = sem("scored"), sem("max_ready"), sem("neg_max")
        exp_done, sink_shifted, sink_done = sem("exp_done"), sem("sink_shifted"), sem("sink_done")
        den_ready, inv_ready, prob_scaled = sem("den_ready"), sem("inv_ready"), sem("prob_scaled")
        turned, pT_ready, pv_done, o_stored = sem("turned"), sem("pT_ready"), sem("pv_done"), sem("o_stored")
        o_hi_ready, o_lo_ready = sem("o_hi_ready"), sem("o_lo_ready")
        first_final, stored = sem("first_final"), sem("stored")

        def above_zero(value):
            return not isinstance(value, int) or value > 0

        def repeat(eng, n, body):
            body(0)
            if n > 1:
                with eng.Fori(1, n) as i:
                    body(i)

        def repeat_or_unroll(eng, n, body, unroll):
            if unroll:
                for i in range(n):
                    body(i)
            else:
                repeat(eng, n, body)

        def first_of(i):
            return isinstance(i, int) and i == 0

        def col(name, n):
            return vec_sb[:, ds(VEC[name][0] + n, 1)]

        def two(ap2, w):
            return ap2.rearrange("p (a b) -> p a b", a=2)

        def slot(j, w):
            return PS[:, 2 * j:2 * j + 2, 0:w // 2]

        def ada_sums(tile, n):
            return PS[:, 5, ds(512 - 4 * N_MOD + 2 * tile, 2 * n)]

        def misc(w, bank=4):
            return PS[:, bank:bank + 2, 0:w // 2]

        def segments(t0, w):
            out = []
            if t0 < LAT:
                out.append((0, min(w, LAT - t0), 0))
            if t0 + w > LAT:
                out.append((max(0, LAT - t0), min(w, t0 + w - LAT), 1))
            return out

        def c_parts(t0, w):
            return [(t0 + o + (PAD if cond else 0), o, n) for o, n, cond in segments(t0, w)]

        def wide_rms(ap, w):
            return ap.unsqueeze(1).to_broadcast([P, KT, w])

        def attn_keys(n):
            window = [b for b in (n - 1, n, n + 1) if 0 <= b < NB]
            masks = {2 + i: (mask_left if b < n else mask_right) for i, b in enumerate(window) if b != n}
            return [LAT // BLK, LAT // BLK + 1] + window, masks

        block = ctx.enter_context(nc.Block())

        @block.sync
        def _(sp):
            sp.dma_start(vec_sb[:], vec).then_inc(const_loaded, 16)
            sp.dma_start(cst[:], consts).then_inc(const_loaded, 16)
            sp.dma_start(bcst[:], bconsts).then_inc(const_loaded, 16)
            sp.dma_start(h[:, :, 0:640], xT[:, :, 0:640]).then_inc(h_loaded[0], 16)
            for j in range(4):
                n = ADA_FIRST // 4
                sp.dma_start(ada_first[:, n * j:n * j + n], adastream[n * j:n * j + n].rearrange("g p k n -> p g k n")).then_inc(ada_begun[j], 16)
            for x in ph:
                if "pairs" not in x:
                    continue
                first = UNIT_AT[x["units"]]

                def load(i, x=x, first=first):
                    q = x["q"] + i
                    for j in range(2):
                        if above_zero(2 * q + j - 1):
                            sp.wait_ge(lo_ready, 2 * q + j - 1)
                        sp.dma_start(raw[:, j], wstream[first + 2 * i + j]).then_inc(loaded[j], 16)
                if x["kind"] == "qkv":
                    for i in range(x["pairs"]):
                        load(i, first=first + 2 * (x["order"][i] - i))
                else:
                    repeat(sp, x["pairs"], load)

        @block.gpsimd
        def _(pool):
            nc.gpsimd.memset(eps_t[:], EPS).then_inc(eps_set, 1)
            pool.wait_ge(ada_used, ADA_FIRST)
            for o in (0, PAD + LAT, 2 * PAD + LAT + CTX):
                last = nc.gpsimd.memset(z[:, :, o:o + PAD], 0.0)
            last.then_inc(pad_set, 1)
            for x in ph:
                if x["kind"] == "glu":
                    if x["chunk"]["t0"] == 0:
                        pool.wait_ge(in_lo, 4 * x["n"])
                    else:
                        pool.wait_ge(dw_even, N_EVEN * KT)
                        pool.wait_ge(mod_ready, 4)

                    def load(i, x=x, n=x["ada_per"], slots=ada_slot[x["chunk"]["t0"] > 0]):
                        for r in range(n):
                            if not first_of(i):
                                pool.wait_ge(ada_used, x["ada"] + n * (i - 1) + r + 1)
                            pool.dma_start(slots[r], adastream[x["ada"] + n * i + r]).then_inc(ada_loaded[r], 16)
                    repeat(pool, 8, load)
                if x["kind"] != "attn":
                    continue
                for g in range(16):
                    G = 16 * x["a"] + g
                    w = len(attn_keys(4 * x["half"] + g // 4)[0]) * BLK
                    pool.wait_ge(inv_ready, G + 1)
                    for hh in range(QPK):
                        pr = prob[g % 2][:, hh, 0:w]
                        nc.gpsimd.tensor_scalar(pr, pr, soft[:, 4, g % 2, hh:hh + 1], 1.0, ALU.mult,
                                                ALU.mult).then_inc(prob_scaled, 1)

        @block.scalar
        def _(act):
            A = nc.scalar.activation

            def split(q, j):
                if isinstance(q, int) and q >= n_pairs:
                    return
                act.wait_ge(loaded[j], 16 * q + 16)
                if above_zero(2 * q + j - 1):
                    act.wait_ge(unit_done, 2 * q + j - 1)
                A(w_hi[:, j], raw[:, j], ACT.Copy).then_inc(hi_ready, 1)

            def squares(x, src, t):
                if above_zero(x["s"]):
                    act.wait_ge(norm_step, x["s"])
                if above_zero(x["n"]):
                    act.wait_ge(in_lo, 4 * x["n"])
                A(t, src, ACT.Square).then_inc(norm_step, 1)

            def root(s, w, bank=4):
                act.wait_ge(norm_step, s)
                A(two(rms[:, 0:w], w), misc(w, bank), ACT.Sqrt, bias=eps_t[:]).then_inc(norm_step, 1)

            def chunk_of(x):
                return x["chunk"]["t0"], x.get("w", x["chunk"]["n"])

            def pre_squares(x):
                t0, w = chunk_of(x)
                t, hs = wide_ap(x["t"], w), h[:, :, t0:t0 + w]
                if x["layer"] == 0 and x["which"] == 0:
                    act.wait_ge(h_loaded[t0 > 0], 16)
                if x["t"] == "c_tail":
                    act.wait_ge(ada_used, ADA_FIRST + KT * ADA_PER[0])
                if x["t"] == "o32" and x["r"]:
                    act.wait_ge(rope_step, 3 * x["r"])
                if above_zero(x["k"]):
                    act.wait_ge(k_lo, x["k"])
                if above_zero(x["v"]):
                    act.wait_ge(v_stored, x["v"])
                squares(x, hs, t)

            def high_part(x, t, m):
                act.wait_ge(in_modulated, 4 * x["n"] + m + 1)
                A(a_hi[:, 2 * m:2 * m + 2, 0:t.shape[2]], t[:, 2 * m:2 * m + 2], ACT.Copy).then_inc(in_hi, 1)

            def pre_tiles(x, m):
                t0, w = chunk_of(x)
                t = wide_ap(x["t"], w)
                act.wait_ge(in_normed, 4 * x["n"] + m + 1)
                if m == 0:
                    act.wait_ge(mod_ready, 2 if x["layer"] == 0 and x["which"] == 0 else 6)
                    last_reader = x["q"] - 4 if "hosted" in x else x["q"]
                    if above_zero(2 * last_reader):
                        act.wait_ge(unit_done, 2 * last_reader)
                for k in (2 * m, 2 * m + 1):
                    for o, n, cnd in segments(t0, w):
                        md = mod[x["layer"]][:, cnd, 24 * x["which"]:24 * x["which"] + 24]
                        last = A(t[:, k, o:o + n], t[:, k, o:o + n], ACT.Identity, scale=md[:, 8 + k:9 + k], bias=md[:, k:k + 1])
                last.then_inc(in_modulated, 1)
                high_part(x, t, m)

            def post_squares(x):
                w = x["chunk"]["n"]
                if x["y"] == "y4":
                    act.wait_ge(y_added, x["d"])
                else:
                    act.wait_ge(evacuated, 2 * x["q"])
                squares(x, wide_ap(x["y"], w), wide_ap(x["t"], w))

            def ln_squares(x):
                act.wait_ge(norm_step, x["s"] + 6)
                for co, o, n in c_parts(*chunk_of(x)):
                    last = A(wide["t3"][:, :, o:o + n], c[:, :, co:co + n], ACT.Square)
                last.then_inc(norm_step, 1)

            def store(x):
                t0, w = chunk_of(x)
                act.wait_ge(norm_step, x["s"] + 9)
                act.dma_start(out[:, :, t0:t0 + w], h[:, :, t0:t0 + w]).then_inc(stored, 16)

            act.wait_ge(const_loaded, 48)
            act.wait_ge(eps_set, 1)
            cond = vec_sb[:, VEC["cond"][0]:VEC["cond"][0] + 16].rearrange("p (k a) -> p k a", a=2)
            A(silu_c[:], cond, ACT.Silu).then_inc(cond_ready, 1)
            act.dma_start(h[:, :, 640:TOK], xT[:, :, 640:TOK]).then_inc(h_loaded[1], 16)
            split(0, 0)
            split(0, 1)
            for x in ph:
                if "hosted" in x:
                    continue
                kind, q0, s, ch = x["kind"], x["q"], x["s"], x.get("chunk")
                if kind in ("pre", "post", "ln"):
                    t0, w = ch["t0"], x.get("w", ch["n"])
                if kind == "pre":
                    pre_squares(x)
                    root(s + 5, w)
                    for m in range(4):
                        pre_tiles(x, m)
                if kind == "post":
                    post_squares(x)
                    root(s + 5, w)
                    if "store" in x:
                        act.wait_ge(first_final, 3)
                        act.dma_start(out[:, 0:KT // 2, t0:t0 + w], h[:, 0:KT // 2, t0:t0 + w]).then_inc(stored, 16)
                        act.wait_ge(norm_step, s + 9)
                        act.dma_start(out[:, KT // 2:KT, t0:t0 + w], h[:, KT // 2:KT, t0:t0 + w]).then_inc(stored, 16)
                if kind == "ln":
                    if "stats_hosted" not in x:
                        ln_squares(x)
                        root(s + 11, w)
                    for m in range(4):
                        act.wait_ge(in_normed, 4 * x["n"] + m + 1)
                        for k in (2 * m, 2 * m + 1):
                            for co, o, n in c_parts(t0, w):
                                last = A(wide["t3"][:, k, o:o + n], c[:, k, co:co + n], ACT.Silu,
                                         scale=col("ln_g", k), bias=col("ln_b", k))
                        last.then_inc(in_modulated, 1)
                        if m == 0:
                            act.wait_ge(unit_done, 2 * q0)
                        high_part(x, wide["t3"][:, :, 0:w], m)
                if kind == "glu":
                    def body(i, x=x):
                        q, g = x["q"] + i, x["g"] + i
                        if above_zero(g):
                            act.wait_ge(glu_done, g)
                        act.wait_ge(unit_done, 2 * q + 1)
                        A(two(ug[:, 0:640], 640), slot(0, 640), ACT.Identity, bias=col("cmb_in", i)).then_inc(evacuated, 1)
                        split(q + 1, 0)
                        act.wait_ge(unit_done, 2 * q + 2)
                        A(two(uv[:, 0:640], 640), slot(1, 640), ACT.Sigmoid, bias=col("cmb_in", 8 + i)).then_inc(evacuated, 1)
                        split(q + 1, 1)
                        for r in range(x["ada_per"]):
                            g = x["ada"] + x["ada_per"] * i + r
                            act.wait_ge(ada_used, g + 1)
                            act.wait_ge(ada_turned, g - 1 if r else g)
                            A(ada_row[:, r % 2], PS[0:2, 6 + r % 2, 0:2 * P], ACT.Copy).then_inc(row_ready, 1)
                    repeat(act, 8, body)
                if kind == "lin":
                    w = ch["n"]
                    y = wide_ap(x["y"], w)
                    head, stats = x.get("head"), x.get("stats")

                    def body(i, x=x, w=w, y=y):
                        q = x["q"] + i
                        for j in range(2):
                            if not (x["after_glu"] and first_of(i) and j == 0):
                                split(q + j, 1 - j)
                            if head and j == 0 and i == 0:
                                post_squares(head)
                            if head and j == 0 and i == 1:
                                root(head["s"] + 5, w)
                            act.wait_ge(unit_done, 2 * q + j + 1)
                            dst = y[:, ds(2 * i + j, 1), 0:w].rearrange("p o (a b) -> p (o a) b", a=2)
                            if x["units"] == "cm_out":
                                A(dst, slot(j, w), ACT.Identity, bias=col("b_out", 2 * i + j)).then_inc(evacuated, 1)
                            else:
                                A(dst, slot(j, w), ACT.Copy).then_inc(evacuated, 1)
                        if stats and i == 1:
                            ln_squares(stats)
                        if stats and i == 3:
                            root(stats["s"] + 11, w)
                    if x["units"] == "w_o":
                        act.wait_ge(o_stored, 64)
                        if x["half"]:
                            act.wait_ge(unit_done, 2 * q0)
                        A(o_hi[:], o_out[x["half"]][:], ACT.Copy).then_inc(o_hi_ready, 1)
                    repeat_or_unroll(act, 4, body, head or stats)
                if kind == "ffn":
                    w, n_out = x["w"], ch["n"]
                    q, p, d = x["q"], x["p"], x["d"]
                    head, tail = x.get("head"), x.get("tail")
                    for gi, (f0, nf) in enumerate(GROUPS):
                        def zh(p, i):
                            act.wait_ge(prod_done, p + 1)
                            A(z_hi[:, ds(i, 1), 0:n_out], cv[:, 0:n_out].unsqueeze(1), ACT.Copy).then_inc(zh_done, 1)

                        def up(i, q=q, p=p, d=d):
                            q, p = q + i, p + i
                            split(q, 1)
                            if above_zero(3 * p):
                                act.wait_ge(gate_conv, 3 * p)
                            if first_of(i):
                                if above_zero(d):
                                    act.wait_ge(y_added, d)
                            act.wait_ge(unit_done, 2 * q + 1)
                            A(two(ug[:, 0:w], w), slot(0, w), ACT.Copy).then_inc(evacuated, 1)
                            if not first_of(i):
                                zh(p - 1, i - 1)
                            split(q + 1, 0)
                            if above_zero(3 * p):
                                act.wait_ge(val_conv, 3 * p)
                            act.wait_ge(unit_done, 2 * q + 2)
                            A(two(uv[:, 0:w], w), slot(1, w), ACT.Copy).then_inc(evacuated, 1)
                            act.wait_ge(gate_conv, 3 * p + 3)
                            A(cg[:, 0:n_out], cg[:, 0:n_out], ACT.Silu).then_inc(silu_done, 1)
                            if head and gi == 0 and i == 0:
                                post_squares(head)
                            if head and gi == 0 and i == 3:
                                root(head["s"] + 5, head["chunk"]["n"])
                        repeat_or_unroll(act, nf, up, head and gi == 0)
                        q, p = q + nf, p + nf
                        zh(p - 1, nf - 1)

                        def down(i, q=q, p=p, d=d, gi=gi):
                            q = q + i
                            for j in range(2):
                                split(q + j, 1 - j)
                                if tail and gi == 2 and j == 1:
                                    pre_tiles(tail, i)
                                if head and gi == 0 and first_of(i) and j == 0:
                                    act.wait_ge(norm_step, head["s"] + 9)
                                    if "store" in head:
                                        store(head)
                                act.wait_ge(unit_done, 2 * q + j + 1)
                                if gi == 0:
                                    dst = wide["y4"][:, ds(2 * i + j, 1), 0:n_out].rearrange("p o (a b) -> p (o a) b", a=2)
                                else:
                                    if above_zero(d + 2 * i + j - 1):
                                        act.wait_ge(y_added, d + 2 * i + j - 1)
                                    if first_of(i) and j == 0:
                                        act.wait_ge(zl_done, p)
                                    dst = two((ug, uv)[j][:, 0:n_out], n_out)
                                A(dst, slot(j, n_out), ACT.Copy).then_inc(evacuated, 1)
                            if tail and gi == 1 and i == 0:
                                pre_squares(tail)
                            if tail and gi == 1 and i == 2:
                                root(tail["s"] + 5, tail["w"])
                        if q + 4 == n_pairs:
                            repeat(act, 3, down)
                            down(3)
                        else:
                            repeat_or_unroll(act, 4, down, tail and gi > 0)
                        q += 4
                        if gi:
                            d += KT
                if kind == "qkv":
                    w, t0 = ch["n"], ch["t0"]
                    head = x.get("head")
                    if head:
                        act.wait_ge(y_added, x["d"])
                        act.dma_start(rope_sb[:], rope).then_inc(rope_loaded, 16)
                    for i in range(x["pairs"]):
                        q = q0 + i
                        for j in range(2):
                            u = x["list"][2 * i + j]
                            split(q + j, 1 - j)
                            if head and i == 0 and j == 0:
                                post_squares(head)
                            if head and i == 1 and j == 0:
                                root(head["s"] + 5, head["chunk"]["n"], 6)
                            if head and i == 4 and j == 0:
                                act.wait_ge(norm_step, s)
                            if u["free"] and u["free"][0] == "rope":
                                act.wait_ge(rope_step, u["free"][1])
                            if u["free"] and u["free"][0] == "k_lo":
                                act.wait_ge(k_lo, u["free"][1])
                            if u["free"] and u["free"][0] == "v_turned":
                                act.wait_ge(v_turned, u["free"][1])
                            if i == 0 and j == 0 and not head:
                                act.wait_ge(norm_step, s)
                            act.wait_ge(unit_done, 2 * q + j + 1)
                            A(two(rb[j][:, 0:w], w), slot(j, w), ACT.Copy).then_inc(evacuated, 1)
                        for j in range(2):
                            u = x["list"][2 * i + j]
                            g = 2 * u["tile"]
                            if u["kind"] == "k":
                                if u["roped"]:
                                    act.wait_ge(rope_step, 3 * u["r"] + 3)
                                else:
                                    act.wait_ge(evacuated, 2 * q + j + 1)
                                src = tb[j] if u["roped"] else rb[j]
                                A(ks[0:64, g, t0:t0 + w], src[0:64, 0:w], ACT.Copy)
                                A(ks[64:128, g + 1, t0:t0 + w], src[64:128, 0:w], ACT.Copy)
                                A(ks[0:64, g + 1, t0:t0 + w], src[64:128, 0:w], ACT.Copy).then_inc(k_hi, 1)
                            if u["kind"] == "v":
                                act.wait_ge(v_turned, u["v"] + 1)
                                A(v_sb[:, t0 // BLK:(t0 + w) // BLK, u["tile"] * P:(u["tile"] + 1) * P],
                                  PS[:, 6 + j, 0:w].rearrange("p (a b) -> p a b", b=P), ACT.Copy).then_inc(v_stored, 1)
                if kind == "attn":
                    a0, half = x["a"], x["half"]

                    def cut(g, part):
                        if above_zero(64 * a0 + 4 * (g - 3)):
                            act.wait_ge(scored, 64 * a0 + 4 * (g - 3))
                        if g == 0 and part == 0:
                            act.wait_ge(norm_step, s)
                            act.wait_ge(rope_step, 3 * x["r"])
                            act.wait_ge(k_lo, x["k"])
                            act.wait_ge(unit_done, 2 * q0)
                        cb, kv = (g // 4) * BLK, g % 4
                        sh = part // 2 * 64
                        dh = sh if part % 2 == 0 else 64 - sh
                        A(qs_hi[dh:dh + 64, 4 * kv + part // 2:4 * kv + 4:2, :], qh[half][sh:sh + 64, 2 * kv:2 * kv + 2, cb:cb + BLK],
                          ACT.Copy, scale=HD ** -0.5).then_inc(qs_cut, 1)

                    for g in range(3):
                        for part in range(4):
                            cut(g, part)
                    for n in range(64 + LAG):
                        g, hh, m = n // QPK, n % QPK, n - LAG
                        if m >= 0:
                            nk = len(attn_keys(4 * half + m // 16)[0])
                            act.wait_ge(turned, 64 * a0 + m + 1)
                            if above_zero(32 * a0 + m // 2 - 1):
                                act.wait_ge(pv_done, 32 * a0 + m // 2 - 1)
                            if m == 0 and a0 == 0:
                                act.wait_ge(rope_step, 3 * x["r"])
                            A(pT[:, 0:nk, m % QPK * BLK:(m % QPK + 1) * BLK],
                              PS[:, 4:6, :].rearrange("p a b -> p (a b)")[:, 0:nk * BLK].rearrange("p (a b) -> p a b", b=BLK),
                              ACT.Copy).then_inc(pT_ready, 1)
                        if n < 64:
                            N = 64 * a0 + n
                            w = len(attn_keys(4 * half + g // 4)[0]) * BLK
                            act.wait_ge(neg_max, N + 1)
                            if above_zero(N - 7):
                                act.wait_ge(turned, N - 7)
                            A(prob[g % 2][:, hh, 0:w], PS[:, 2 * (hh % 2):2 * (hh % 2) + 2, :].rearrange("p a b -> p (a b)")[:, 0:w],
                              ACT.Exp, bias=soft[:, 1, g % 2, hh:hh + 1], accum_out=soft[:, 2, g % 2, hh:hh + 1]).then_inc(exp_done, 1)
                            if hh == QPK - 1:
                                act.wait_ge(sink_shifted, 16 * a0 + g + 1)
                                A(soft[:, 3, g % 2, :], soft[:, 3, g % 2, :], ACT.Exp).then_inc(sink_done, 1)
                            if g + 3 < 16:
                                cut(g + 3, hh)
            act.wait_ge(stored, 48)

        @block.vector
        def _(dve):
            TT, TS, STT = nc.vector.tensor_tensor, nc.vector.tensor_scalar, nc.vector.scalar_tensor_tensor

            def split(q, j):
                if isinstance(q, int) and q >= n_pairs:
                    return
                dve.wait_ge(hi_ready, 2 * q + j + 1)
                TT(w_lo[:, j], raw[:, j], w_hi[:, j].bitcast(F32), ALU.subtract).then_inc(lo_ready, 1)

            def sum_tiles(s, t):
                for i, n in enumerate((4, 2, 1)):
                    dve.wait_ge(norm_step, s + i)
                    TT(t[:, 0:n], t[:, 0:n], t[:, n:2 * n], ALU.add).then_inc(norm_step, 1)

            def invert(s, w):
                dve.wait_ge(norm_step, s)
                nc.vector.reciprocal(rms[:, 0:w], rms[:, 0:w]).then_inc(norm_step, 1)

            def modulation(x):
                l, f0, f1, ready = x["layer"], x["first"], x["last"], x["ready"]
                at_b, at_g = VEC[f"ada_b{l}"][0], VEC["norm_g"][0] + 32 * l
                dve.wait_ge(ada_turned, x["used"])
                for cnd in range(2):
                    sums = ada_sums(N_MOD * l + f0, f1 - f0).rearrange("p (f a) -> p a f", a=2)[:, cnd, :]
                    last = TT(mod[l][:, cnd, f0:f1], sums, vec_sb[:, at_b + f0:at_b + f1], ALU.add)
                last.then_inc(mod_ready, 1)
                dve.wait_ge(mod_ready, ready + 1)
                for cnd in range(2):
                    for which in range(2):
                        m = mod[l][:, cnd, 24 * which:24 * which + 24]
                        g = at_g + 16 * which
                        if f0 <= 24 * which + 8 < f1:
                            last = STT(m[:, 8:16], m[:, 8:16], 1.0, vec_sb[:, g:g + 8], ALU.add, ALU.mult)
                        if f0 <= 24 * which + 16 < f1:
                            last = TT(m[:, 16:24], m[:, 16:24], vec_sb[:, g + 8:g + 16], ALU.mult)
                last.then_inc(mod_ready, 1)
                dve.wait_ge(mod_ready, ready + 2)

            def pre_normed(x, m):
                t0, w = x["chunk"]["t0"], x["w"]
                dve.wait_ge(norm_step, x["s"] + 7)
                TT(wide_ap(x["t"], w)[:, 2 * m:2 * m + 2], h[:, 2 * m:2 * m + 2, t0:t0 + w],
                   rms[:, 0:w].unsqueeze(1).to_broadcast([P, 2, w]), ALU.mult).then_inc(in_normed, 1)

            def remainder(x, t, m):
                w = t.shape[2]
                dve.wait_ge(in_hi, 4 * x["n"] + m + 1)
                TT(a_lo[:, 2 * m:2 * m + 2, 0:w], t[:, 2 * m:2 * m + 2], a_hi[:, 2 * m:2 * m + 2, 0:w].bitcast(F32),
                   ALU.subtract).then_inc(in_lo, 1)

            def ln_mean_sum(x):
                t3, (t0, w) = wide["t3"], (x["chunk"]["t0"], x["chunk"]["n"])
                dve.wait_ge(dw_even, N_EVEN * 2 * KT)
                dve.wait_ge(norm_step, x["s"])
                dve.wait_ge(in_lo, 4 * x["n"])
                for co, o, n in c_parts(t0, w):
                    last = TT(t3[:, 0:4, o:o + n], c[:, 0:4, co:co + n], c[:, 4:8, co:co + n], ALU.add)
                last.then_inc(norm_step, 1)
                for i, m in enumerate((2, 1)):
                    dve.wait_ge(norm_step, x["s"] + 1 + i)
                    TT(t3[:, 0:m, 0:w], t3[:, 0:m, 0:w], t3[:, m:2 * m, 0:w], ALU.add).then_inc(norm_step, 1)

            def ln_centre(x):
                t0, w = x["chunk"]["t0"], x["chunk"]["n"]
                dve.wait_ge(norm_step, x["s"] + 4)
                nc.vector.tensor_copy(two(rms[:, 0:w], w), misc(w)).then_inc(norm_step, 1)
                dve.wait_ge(norm_step, x["s"] + 5)
                for co, o, n in c_parts(t0, w):
                    last = TT(c[:, :, co:co + n], c[:, :, co:co + n], wide_rms(rms[:, o:o + n], n), ALU.subtract)
                last.then_inc(norm_step, 1)

            def post_scale(x):
                w = x["chunk"]["n"]
                y = wide_ap(x["y"], w)
                dve.wait_ge(norm_step, x["s"] + 7)
                TT(y, y, wide_rms(rms[:, 0:w], w), ALU.mult).then_inc(norm_step, 1)

            def post_update(x, first, last_k):
                t0, w = x["chunk"]["t0"], x["chunk"]["n"]
                y = wide_ap(x["y"], w)
                dve.wait_ge(norm_step, x["s"] + 8)
                for k in range(first, last_k):
                    for o, n, cnd in segments(t0, w):
                        hk = h[:, k, t0 + o:t0 + o + n]
                        at_gate = 24 * x["which"] + 16 + k
                        last = STT(hk, y[:, k, o:o + n], mod[x["layer"]][:, cnd, at_gate:at_gate + 1], hk, ALU.mult, ALU.add)
                last.then_inc(norm_step if last_k == KT else first_final, 1)

            dve.wait_ge(const_loaded, 48)
            split(0, 0)
            split(0, 1)
            for x in ph:
                if "hosted" in x:
                    continue
                kind, q0, s, ch = x["kind"], x["q"], x["s"], x.get("chunk")
                if kind in ("pre", "post", "ln"):
                    t0, w = ch["t0"], x.get("w", ch["n"])
                if kind == "mod":
                    modulation(x)
                if kind == "pre":
                    t = wide_ap(x["t"], w)
                    sum_tiles(s + 1, t)
                    invert(s + 6, w)
                    if "mod" in x:
                        for m in range(4):
                            pre_normed(x, m)
                        for g in range(ADA_FIRST):
                            dve.wait_ge(ada_used, g + 1)
                            if above_zero(g - 1):
                                dve.wait_ge(ada_turned, g - 1)
                            nc.vector.tensor_copy(ada_row[:, g % 2], PS[0:2, 6 + g % 2, 0:2 * P]).then_inc(row_ready, 1)
                        modulation(x["mod"])
                    for m in range(5):
                        if m < 4 and "mod" not in x:
                            pre_normed(x, m)
                        if m:
                            remainder(x, t, m - 1)
                if kind == "post":
                    sum_tiles(s + 1, wide_ap(x["t"], w))
                    invert(s + 6, w)
                    post_scale(x)
                    if "store" in x:
                        post_update(x, 0, KT // 2)
                        post_update(x, KT // 2, KT)
                    else:
                        post_update(x, 0, KT)
                if kind == "ln":
                    t3 = wide["t3"]
                    if "stats_hosted" not in x:
                        ln_mean_sum(x)
                        ln_centre(x)
                        sum_tiles(s + 7, t3[:, :, 0:w])
                        invert(s + 12, w)
                    dve.wait_ge(norm_step, s + 13)
                    for m in range(5):
                        if m < 4:
                            for co, o, n in c_parts(t0, w):
                                cm = c[:, 2 * m:2 * m + 2, co:co + n]
                                last = TT(cm, cm, rms[:, o:o + n].unsqueeze(1).to_broadcast([P, 2, n]), ALU.mult)
                            last.then_inc(in_normed, 1)
                        if m:
                            remainder(x, t3[:, :, 0:w], m - 1)
                if kind == "glu":
                    first = ch["t0"] == 0
                    o0 = 0 if first else 640 - PAD
                    m = 640 - PAD if first else CC - o0
                    parts = [(PAD, 0, 640)] if first else [(PAD + 640, 0, LAT - 640), (2 * PAD + LAT, LAT - 640, CTX)]

                    def body(i, x=x, parts=parts, o0=o0, m=m):
                        q, g = x["q"] + i, x["g"] + i
                        if first_of(i):
                            dve.wait_ge(pad_set, 1)
                        dve.wait_ge(evacuated, 2 * q + 2)
                        for zo, o, n in parts:
                            last = TT(z[:, ds(i, 1), zo:zo + n], ug[:, o:o + n].unsqueeze(1), uv[:, o:o + n].unsqueeze(1), ALU.mult)
                        last.then_inc(glu_done, 1)
                        split(q + 1, 0)
                        split(q + 1, 1)
                        dve.wait_ge(glu_done, g + 1)
                        even, odd = c[:, ds(i, 1), o0:o0 + m], dw_acc[:, 0:m].unsqueeze(1)
                        for k in range(CW):
                            src, tap = z[:, ds(i, 1), o0 + k:o0 + k + m], col("dw_w", i * CW + k)
                            if k == 0:
                                TS(even, src, tap, col("dw_b", i), ALU.mult, ALU.add).then_inc(dw_even, 1)
                            elif k == 1:
                                if above_zero(N_EVEN * g):
                                    dve.wait_ge(dw_even, N_EVEN * g)
                                TS(odd, src, tap, 0.0, ALU.mult, ALU.add).then_inc(dw_odd, 1)
                            elif k % 2 == 0:
                                dve.wait_ge(dw_even, N_EVEN * g + k // 2)
                                STT(even, src, tap, even, ALU.mult, ALU.add).then_inc(dw_even, 1)
                            else:
                                dve.wait_ge(dw_odd, N_ODD * g + k // 2)
                                STT(odd, src, tap, odd, ALU.mult, ALU.add).then_inc(dw_odd, 1)
                        dve.wait_ge(dw_even, N_EVEN * g + N_EVEN - 1)
                        dve.wait_ge(dw_odd, N_ODD * g + N_ODD)
                        TT(even, even, odd, ALU.add).then_inc(dw_even, 1)
                    repeat(dve, 8, body)
                if kind == "lin":
                    def body(i, x=x):
                        q = x["q"] + i
                        if not (x["after_glu"] and first_of(i)):
                            split(q, 1)
                        split(q + 1, 0)
                        if stats and i == 0:
                            ln_mean_sum(stats)
                        if stats and i == 1:
                            ln_centre(stats)
                        if stats and i == 2:
                            sum_tiles(stats["s"] + 7, wide["t3"][:, :, 0:w])
                        if stats and i == 3:
                            invert(stats["s"] + 12, w)
                        if head and i == 0:
                            sum_tiles(head["s"] + 1, wide_ap(head["t"], w))
                        if head and i == 1:
                            invert(head["s"] + 6, w)
                        if head and i == 2:
                            post_scale(head)
                        if head and i == 3:
                            post_update(head, 0, KT)
                    w, head, stats = ch["n"], x.get("head"), x.get("stats")
                    if x["units"] == "w_o":
                        dve.wait_ge(o_hi_ready, x["half"] + 1)
                        TT(o_lo[:], o_out[x["half"]][:], o_hi[:].bitcast(F32), ALU.subtract).then_inc(o_lo_ready, 1)
                    repeat_or_unroll(dve, 4, body, head or stats)
                if kind == "ffn":
                    n_out, l = ch["n"], x["layer"]
                    head, tail = x.get("head"), x.get("tail")
                    leftmost = ch["t0"] == 0
                    cut_at = LAT - ch["t0"] if ch["t0"] < LAT < ch["t0"] + n_out else None
                    q, p, d = x["q"], x["p"], x["d"]
                    for gi, (f0, nf) in enumerate(GROUPS):
                        def zl(p, i):
                            dve.wait_ge(zh_done, p + 1)
                            TT(z_lo[:, ds(i, 1), 0:n_out], cv[:, 0:n_out].unsqueeze(1), z_hi[:, ds(i, 1), 0:n_out].bitcast(F32),
                               ALU.subtract).then_inc(zl_done, 1)

                        def conv3(u, dst, signal, p, f):
                            tap = [col(f"cw{l}", f * 4 + t) for t in range(4)]
                            edge = u_edge[:, ds(f, 1)]
                            TS(dst[:, 0:n_out], u[:, 0:n_out], tap[1], tap[3], ALU.mult, ALU.add).then_inc(signal, 1)
                            dve.wait_ge(signal, 3 * p + 1)
                            cuts = [(1, n_out)] if cut_at is None else [(1, cut_at), (cut_at + 1, n_out)]
                            if not leftmost:
                                STT(dst[:, 0:1], edge, tap[0], dst[:, 0:1], ALU.mult, ALU.add)
                            for lo, hi in cuts:
                                last = STT(dst[:, lo:hi], u[:, lo - 1:hi - 1], tap[0], dst[:, lo:hi], ALU.mult, ALU.add)
                            last.then_inc(signal, 1)
                            dve.wait_ge(signal, 3 * p + 2)
                            if leftmost:
                                nc.vector.tensor_copy(edge, u[:, n_out - 1:n_out])
                                cuts = [(0, n_out)]
                            else:
                                cuts = [(0, n_out - 1)] if cut_at is None else [(0, cut_at - 1), (cut_at, n_out - 1)]
                            for lo, hi in cuts:
                                last = STT(dst[:, lo:hi], u[:, lo + 1:hi + 1], tap[2], dst[:, lo:hi], ALU.mult, ALU.add)
                            last.then_inc(signal, 1)

                        def up(i, q=q, p=p, f0=f0):
                            q, p = q + i, p + i
                            split(q, 1)
                            if above_zero(p):
                                dve.wait_ge(prod_done, p)
                            dve.wait_ge(evacuated, 2 * q + 1)
                            conv3(ug, cg, gate_conv, p, f0 + i)
                            if not first_of(i):
                                zl(p - 1, i - 1)
                            split(q + 1, 0)
                            if above_zero(p):
                                dve.wait_ge(zl_done, p)
                            dve.wait_ge(evacuated, 2 * q + 2)
                            conv3(uv, cv, val_conv, p, f0 + i + FT)
                            dve.wait_ge(silu_done, p + 1)
                            dve.wait_ge(val_conv, 3 * p + 3)
                            TT(cv[:, 0:n_out], cg[:, 0:n_out], cv[:, 0:n_out], ALU.mult).then_inc(prod_done, 1)
                            if head and gi == 0:
                                if i == 1:
                                    sum_tiles(head["s"] + 1, wide_ap(head["t"], head["chunk"]["n"]))
                                if i == 4:
                                    invert(head["s"] + 6, head["chunk"]["n"])
                                if i == 5:
                                    post_scale(head)
                                if i >= 6:
                                    post_update(head, 4 * (i - 6), 4 * (i - 5))
                            if tail and gi == 2 and first_of(i):
                                for m in range(4):
                                    pre_normed(tail, m)
                        repeat_or_unroll(dve, nf, up, head and gi == 0)
                        q, p = q + nf, p + nf
                        zl(p - 1, nf - 1)

                        def down(i, q=q, d=d, gi=gi):
                            q = q + i
                            for j in range(2):
                                split(q + j, 1 - j)
                                if gi:
                                    dve.wait_ge(evacuated, 2 * q + j + 1)
                                    if gi == 2:
                                        dve.wait_ge(y_added, d + 2 * i + j - 7)
                                    yk = wide["y4"][:, ds(2 * i + j, 1), 0:n_out]
                                    TT(yk, (ug, uv)[j][:, 0:n_out].unsqueeze(1), yk, ALU.add).then_inc(y_added, 1)
                            if tail and gi == 1 and i == 1:
                                sum_tiles(tail["s"] + 1, wide_ap(tail["t"], tail["w"]))
                            if tail and gi == 1 and i == 3:
                                invert(tail["s"] + 6, tail["w"])
                            if tail and gi == 2:
                                for m in range(max(0, i - 1), i + (i == 3)):
                                    remainder(tail, wide_ap(tail["t"], tail["w"]), m)
                        if q + 4 == n_pairs:
                            repeat(dve, 3, down)
                            down(3)
                        else:
                            repeat_or_unroll(dve, 4, down, tail and gi > 0)
                        q += 4
                        if gi:
                            d += KT
                if kind == "qkv":
                    w, t0 = ch["n"], ch["t0"]
                    head = x.get("head")
                    if head:
                        dve.wait_ge(rope_loaded, 16)
                    for i in range(x["pairs"]):
                        q = q0 + i
                        for j in range(2):
                            split(q + j, 1 - j)
                        for j in range(2):
                            u = x["list"][2 * i + j]
                            g = 2 * u["tile"]
                            r3 = 3 * u["r"]
                            if u["roped"]:
                                dve.wait_ge(evacuated, 2 * q + j + 1)
                                if above_zero(u["k"]):
                                    dve.wait_ge(k_hi, u["k"])
                                    dve.wait_ge(k_lo, u["k"])
                                if above_zero(r3):
                                    dve.wait_ge(rope_step, r3)
                                TT(tb[j][:, 0:w], rb[j][:, 0:w], rope_sb[:, 0, t0:t0 + w], ALU.mult).then_inc(rope_step, 1)
                                dve.wait_ge(rot_done, u["r"] + 1)
                                dve.wait_ge(rope_step, r3 + 1)
                                TT(rb[j][:, 0:w], PS[:, 4 + j, 0:w], rope_sb[:, 1, t0:t0 + w], ALU.mult).then_inc(rope_step, 1)
                                dve.wait_ge(rope_step, r3 + 2)
                                dst = tb[j][:, 0:w] if u["kind"] == "k" else qh[t0 // 512][:, u["tile"], 0:w]
                                TT(dst, tb[j][:, 0:w], rb[j][:, 0:w], ALU.add).then_inc(rope_step, 1)
                            if u["kind"] == "k":
                                dve.wait_ge(k_hi, u["k"] + 1)
                                src = tb[j] if u["roped"] else rb[j]
                                TT(ks[64:128, g, t0:t0 + w], src[0:64, 0:w], ks[0:64, g, t0:t0 + w].bitcast(F32), ALU.subtract)
                                TT(ks[64:128, g + 1, t0:t0 + w], src[64:128, 0:w], ks[64:128, g + 1, t0:t0 + w].bitcast(F32),
                                   ALU.subtract).then_inc(k_lo, 1)
                        if head and i == 0:
                            sum_tiles(head["s"] + 1, wide_ap(head["t"], head["chunk"]["n"]))
                        if head and i == 1:
                            invert(head["s"] + 6, head["chunk"]["n"])
                        if head and i == 2:
                            post_scale(head)
                        if head and i == 3:
                            post_update(head, 0, KT)
                if kind == "attn":
                    a0, half = x["a"], x["half"]

                    def cut(g, part):
                        dve.wait_ge(qs_cut, 64 * a0 + 4 * g + part + 1)
                        cb, kv = (g // 4) * BLK, g % 4
                        sh = part // 2 * 64
                        dh = sh if part % 2 == 0 else 64 - sh
                        heads = slice(4 * kv + part // 2, 4 * kv + 4, 2)
                        STT(qs_lo[dh:dh + 64, heads, :], qh[half][sh:sh + 64, 2 * kv:2 * kv + 2, cb:cb + BLK], HD ** -0.5,
                            qs_hi[sh:sh + 64, heads, :].bitcast(F32), ALU.mult, ALU.subtract).then_inc(qs_ready, 1)

                    for g in range(3):
                        for part in range(4):
                            cut(g, part)
                    for n in range(64 + LAG + 3):
                        g, hh, H = n // QPK, n % QPK, (n - LAG - 4) // 2
                        if H >= 0 and (n - LAG) % 2 == 0:
                            tile, cb = H // 2 % 4 * 2 + H % 2, H // 8 * BLK
                            dve.wait_ge(pv_done, 32 * a0 + H + 1)
                            nc.vector.tensor_copy(o_out[half][0:64, tile, cb:cb + BLK], PS[0:64, 6 + H % 2, 0:BLK])
                            nc.vector.tensor_copy(o_out[half][64:128, tile, cb:cb + BLK], PS[0:64, 6 + H % 2, BLK:2 * BLK]).then_inc(o_stored, 1)
                        if n < 64:
                            N, G = 64 * a0 + n, 16 * a0 + g
                            w = len(attn_keys(4 * half + g // 4)[0]) * BLK
                            dve.wait_ge(scored, N + 1)
                            if above_zero(N - 7):
                                dve.wait_ge(neg_max, N - 7)
                            nc.vector.reduce_max(soft[:, 0, g % 2, hh:hh + 1],
                                                 PS[:, 2 * (hh % 2):2 * (hh % 2) + 2, :].rearrange("p a b -> p (a b)")[:, 0:w],
                                                 AX_X).then_inc(max_ready, 1)
                            dve.wait_ge(max_ready, N + 1)
                            if above_zero(N - 7):
                                dve.wait_ge(exp_done, N - 7)
                            if above_zero(G - 1):
                                dve.wait_ge(sink_shifted, G - 1)
                            TS(soft[:, 1, g % 2, hh:hh + 1], soft[:, 0, g % 2, hh:hh + 1], col("sink", 4 * (g % 4) + hh), -1.0,
                               ALU.max, ALU.mult).then_inc(neg_max, 1)
                            if hh == QPK - 1:
                                at_sink = VEC["sink"][0] + 4 * (g % 4)
                                dve.wait_ge(neg_max, N + 1)
                                if above_zero(G - 1):
                                    dve.wait_ge(den_ready, G - 1)
                                TT(soft[:, 3, g % 2, :], vec_sb[:, at_sink:at_sink + QPK], soft[:, 1, g % 2, :], ALU.add).then_inc(sink_shifted, 1)
                        if n % QPK == 0 and 0 < n <= 64:
                            G, b = 16 * a0 + g - 1, (g - 1) % 2
                            dve.wait_ge(sink_done, G + 1)
                            TT(soft[:, 2, b, :], soft[:, 2, b, :], soft[:, 3, b, :], ALU.add).then_inc(den_ready, 1)
                            dve.wait_ge(den_ready, G + 1)
                            if above_zero(4 * (G - 1)):
                                dve.wait_ge(prob_scaled, 4 * (G - 1))
                            nc.vector.reciprocal(soft[:, 4, b, :], soft[:, 2, b, :]).then_inc(inv_ready, 1)
                        if 0 < n <= 52:
                            cut((n - 1) // 4 + 3, (n - 1) % 4)

        @block.tensor
        def _(pe):
            MM = nc.tensor.matmul

            def unit(q, j, hi, lo, w, tiles, before_last=None):
                pe.wait_ge(lo_ready, 2 * q + j + 1)
                if above_zero(2 * q + j - 1):
                    pe.wait_ge(evacuated, 2 * q + j - 1)
                n = w // 2
                for k in range(tiles):
                    if k == tiles - 1 and before_last:
                        before_last()
                    for p_, (wt, mv) in enumerate(((w_hi, hi), (w_hi, lo), (w_lo, hi))):
                        for m in range(2):
                            last = MM(PS[:, 2 * j + m, 0:n], wt[:, j, k, :], mv[:, k, m * n:(m + 1) * n],
                                      start=(k == 0 and p_ == 0), stop=(k == tiles - 1 and p_ == 2))
                last.then_inc(unit_done, 1)

            def average(s, t0_ap, w, bank=4):
                pe.wait_ge(norm_step, s)
                n = w // 2
                for m in range(2):
                    last = MM(PS[:, bank + m, 0:n], ones, t0_ap[:, m * n:(m + 1) * n], start=True, stop=True)
                last.then_inc(norm_step, 1)

            def ada_rows(g, weights, b):
                for k in range(KT):
                    last = MM(PS[0:2, 6 + b, 0:2 * P], silu_c[:, k, :], weights[:, k, :], start=(k == 0), stop=(k == KT - 1))
                last.then_inc(ada_used, 1)

            def ada_turn(g, b):
                pe.wait_ge(row_ready, g + 1)
                for r in range(2):
                    last = MM(ada_sums(2 * g + r, 1), ada_row[:, b, r * P:(r + 1) * P], ident[0:2, 0:2], start=True, stop=True)
                last.then_inc(ada_turned, 1)

            pe.wait_ge(const_loaded, 48)
            pe.wait_ge(cond_ready, 1)
            for x in ph:
                if "hosted" in x:
                    continue
                kind, q0, s, ch = x["kind"], x["q"], x["s"], x.get("chunk")
                if kind in ("pre", "post", "ln"):
                    t0, w = ch["t0"], x.get("w", ch["n"])
                if kind == "ada":
                    for g in range(ADA_FIRST):
                        if g % 2 == 0:
                            pe.wait_ge(ada_begun[g // 2], 16)
                        if above_zero(g - 1):
                            pe.wait_ge(row_ready, g - 1)
                        ada_rows(g, ada_first[:, g], g % 2)
                        if g == 1:
                            pe.wait_ge(norm_step, 6)
                        if g:
                            ada_turn(g - 1, (g - 1) % 2)
                    ada_turn(ADA_FIRST - 1, (ADA_FIRST - 1) % 2)
                if kind in ("pre", "post"):
                    average(s + 4, wide_ap(x["t"], w)[:, 0], w)
                if kind == "ln" and "stats_hosted" not in x:
                    average(s + 3, wide["t3"][:, 0], w)
                    average(s + 10, wide["t3"][:, 0], w)
                if kind in ("glu", "ffn", "qkv"):
                    pe.wait_ge(in_lo, 4 * x["n"])
                if kind == "glu":
                    def body(i, x=x):
                        for j in range(2):
                            unit(x["q"] + i, j, a_hi, a_lo, 640, KT)
                        for r, slot_r in enumerate(ada_slot[x["chunk"]["t0"] > 0]):
                            before = KT if x["chunk"]["t0"] > 0 else 0
                            pe.wait_ge(ada_loaded[r], 16 * (i + 1 + before))
                            g = x["ada"] + x["ada_per"] * i + r
                            if r > 1:
                                pe.wait_ge(row_ready, g - 1)
                            ada_rows(g, slot_r, r % 2)
                            if r:
                                ada_turn(g - 1, (r - 1) % 2)
                        ada_turn(x["ada"] + x["ada_per"] * (i + 1) - 1, (x["ada_per"] - 1) % 2)
                    repeat(pe, 8, body)
                if kind == "lin":
                    if x["units"] == "cm_out":
                        pe.wait_ge(in_lo, 4 * x["n"])
                    else:
                        pe.wait_ge(o_lo_ready, x["half"] + 1)
                    hi, lo = (a_hi, a_lo) if x["units"] == "cm_out" else (o_hi, o_lo)
                    head, stats = x.get("head"), x.get("stats")

                    def body(i, x=x, hi=hi, lo=lo, w=ch["n"]):
                        if stats and i == 1:
                            average(stats["s"] + 3, wide["t3"][:, 0], w)
                        if stats and i == 3:
                            average(stats["s"] + 10, wide["t3"][:, 0], w)
                        if head and i == 1:
                            average(head["s"] + 4, wide_ap(head["t"], w)[:, 0], w)
                        for j in range(2):
                            unit(x["q"] + i, j, hi, lo, w, KT)
                    repeat_or_unroll(pe, 4, body, head or stats)
                if kind == "ffn":
                    q, p = x["q"], x["p"]
                    head, tail = x.get("head"), x.get("tail")
                    for gi, (f0, nf) in enumerate(GROUPS):
                        def up(i, q=q, w=x["w"]):
                            if head and gi == 0 and i == 3:
                                average(head["s"] + 4, wide_ap(head["t"], head["chunk"]["n"])[:, 0], head["chunk"]["n"])
                            for j in range(2):
                                unit(q + i, j, a_hi, a_lo, w, KT)
                        repeat_or_unroll(pe, nf, up, head and gi == 0)
                        q, p = q + nf, p + nf

                        def z_whole(p=p):
                            pe.wait_ge(zl_done, p)

                        def down(i, q=q, p=p, nf=nf, n=ch["n"]):
                            if tail and gi == 1 and i == 2:
                                average(tail["s"] + 4, wide_ap(tail["t"], tail["w"])[:, 0], tail["w"])
                            for j in range(2):
                                if first_of(i) and j == 0:
                                    pe.wait_ge(zl_done, p - 1)
                                unit(q + i, j, z_hi, z_lo, n, nf, z_whole if first_of(i) and j == 0 else None)
                        repeat_or_unroll(pe, 4, down, tail and gi == 1)
                        q += 4
                if kind == "qkv":
                    w, t0 = ch["n"], ch["t0"]
                    head = x.get("head")
                    for i in range(x["pairs"]):
                        q = q0 + i
                        if head and i == 1:
                            average(head["s"] + 4, wide_ap(head["t"], head["chunk"]["n"])[:, 0], head["chunk"]["n"], 6)
                        for j in range(2):
                            unit(q, j, a_hi, a_lo, w, KT)
                        for j in range(2):
                            u = x["list"][2 * i + j]
                            pe.wait_ge(evacuated, 2 * q + j + 1)
                            if u["roped"]:
                                if above_zero(3 * (u["r"] - 1)):
                                    pe.wait_ge(rope_step, 3 * (u["r"] - 1))
                                MM(PS[:, 4 + j, 0:w], rot, rb[j][:, 0:w], start=True, stop=True).then_inc(rot_done, 1)
                            if u["kind"] == "v":
                                if above_zero(u["v"] - 1):
                                    pe.wait_ge(v_stored, u["v"] - 1)
                                for b in range(w // BLK):
                                    last = nc.tensor.transpose(PS[:, 6 + j, b * BLK:(b + 1) * BLK], rb[j][:, b * BLK:(b + 1) * BLK], ident)
                                last.then_inc(v_turned, 1)
                if kind == "attn":
                    a0, half = x["a"], x["half"]

                    def scores(n):
                        g, hh, N = n // QPK, n % QPK, 64 * a0 + n
                        blk = 4 * half + g // 4
                        kv, head = g % 4, 4 * (g % 4) + hh
                        tiles, masks = attn_keys(blk)
                        wt = len(tiles)
                        pe.wait_ge(qs_ready, 64 * a0 + 4 * g + 4)
                        pe.wait_ge(k_lo, x["k"])
                        if above_zero(N - 1):
                            pe.wait_ge(exp_done, N - 1)
                        w0 = tiles[2] * BLK
                        pieces = [(0, 2, LAT), (2, 4, w0)] + [(4, 5, w0 + 2 * BLK)] * (wt == 5)
                        for c0, c1, src in pieces:
                            bank, o = 2 * (hh % 2) + c0 // 4, c0 % 4 * BLK
                            m = (c1 - c0) * BLK
                            masked = [c_ for c_ in range(c0, c1) if c_ in masks]
                            keys = ks[:, kv, src:src + m]
                            MM(PS[:, bank, o:o + m], qs_hi[:, head, :], keys, start=True, stop=False)
                            last = MM(PS[:, bank, o:o + m], qs_lo[:, head, :], keys, start=False, stop=not masked)
                            for c_ in masked:
                                mo = o + (c_ - c0) * BLK
                                last = MM(PS[:, bank, mo:mo + BLK], b_ident, masks[c_], start=False, stop=True)
                        last.then_inc(scored, 1)

                    def turn(m):
                        nk = len(attn_keys(4 * half + m // 16)[0])
                        pe.wait_ge(prob_scaled, 64 * a0 + m + 1)
                        if above_zero(64 * a0 + m):
                            pe.wait_ge(pT_ready, 64 * a0 + m)
                        for t in range(nk):
                            last = nc.tensor.transpose(PS[:, 4 + t // 4, t % 4 * BLK:(t % 4 + 1) * BLK],
                                                       prob[m // QPK % 2][:, m % QPK, t * BLK:(t + 1) * BLK], ident)
                        last.then_inc(turned, 1)

                    def values(H):
                        kv = H // 2 % 4
                        tiles, _ = attn_keys(4 * half + H // 8)
                        pe.wait_ge(pT_ready, 64 * a0 + 2 * H + 2)
                        pe.wait_ge(v_stored, x["v"])
                        if above_zero(32 * a0 + H - 1):
                            pe.wait_ge(o_stored, 32 * a0 + H - 1)
                        for t, tile in enumerate(tiles):
                            last = MM(PS[0:64, 6 + H % 2, 0:2 * BLK], v_sb[:, tile, kv * HD:(kv + 1) * HD],
                                      pT[:, t, H % 2 * 2 * BLK:(H % 2 + 1) * 2 * BLK], start=(t == 0), stop=(t == len(tiles) - 1))
                        last.then_inc(pv_done, 1)

                    scores(0)
                    for n in range(64 + LAG + 1):
                        if LAG <= n < 64 + LAG:
                            turn(n - LAG)
                        if n + 1 < 64:
                            scores(n + 1)
                        if n >= LAG + 2 and (n - LAG) % 2 == 0:
                            values((n - LAG - 2) // 2)


def shape_constants():
    consts = np.zeros((P, 3, P), np.float32)
    consts[:, 0] = 1.0 / D
    consts[:, 1] = np.eye(P)
    for m in range(P):
        if m % 32 < 16:
            consts[m + 16, 2, m] = -1.0
        else:
            consts[m - 16, 2, m] = 1.0
    i, j = np.arange(P)[:, None], np.arange(P)[None, :]
    b = np.zeros((P, 3, P), np.float32)
    b[:, 0] = np.eye(P)
    b[:, 1] = np.where(j < i, NEG, 0.0)
    b[:, 2] = np.where(j > i, NEG, 0.0)
    t = np.arange(LAT)
    inv = (np.float32(10000.0) ** (-np.arange(0, HD // 2, 2, dtype=np.float32) / np.float32(HD // 2))).astype(np.float32)
    row, colm = (t // 64).astype(np.float32), (t % 64).astype(np.float32)
    ar, ac = row[None, :] * inv[:, None], colm[None, :] * inv[:, None]
    ang = np.concatenate([ar, ar, ac, ac] * 2, axis=0).astype(np.float32)
    rope = np.stack([np.cos(ang), np.sin(ang)], axis=1).astype(np.float32)
    return consts, b, np.ascontiguousarray(rope)


def tiles_of(w, cols):
    k = w.shape[0] // P
    v = w.reshape(k, P, w.shape[1] // P, P)
    return [v[:, :, f, :].transpose(1, 0, 2) for f in cols]


def kernel(**inputs):
    import ml_dtypes
    import concourse.bacc as bacc
    from concourse.bass_utils import run_bass_kernel_spmd

    x = {k: np.asarray(v) for k, v in inputs.items()}

    def ffn_units(l):
        up, down = x["ffn_w_up"][l], x["ffn_w_down"][l]
        dv = down.reshape(FT, P, KT, P)
        units = []
        for f0, nf in GROUPS:
            for f in range(f0, f0 + nf):
                units += tiles_of(up, [f, FT + f])
            rows = list(range(f0, f0 + nf)) + [f0] * (8 - nf)
            units += [dv[rows][:, :, n, :].transpose(1, 0, 2) for n in range(KT)]
        return units

    units = tiles_of(x["cm_w_in"][0], [f for i in range(8) for f in (i, 8 + i)])
    units += tiles_of(x["cm_w_out"][0], range(8))
    units += ffn_units(0)
    units += tiles_of(x["attn_w_qkv"][0], [8, 9, 10, 11, 0, 1, 2, 3, 4, 5, 6, 7])
    units += tiles_of(x["attn_w_o"][0], range(8))
    units += ffn_units(1)
    wstream = np.stack(units)
    ada = [np.stack(tiles_of(x["ada_w"][l], range(N_MOD))).reshape(N_MOD // 2, 2, P, KT, P).transpose(0, 2, 3, 1, 4) for l in range(2)]
    adastream = np.concatenate(ada).reshape(N_MOD, P, KT, 2 * P)

    def cols(v):
        return np.ascontiguousarray(v.reshape(-1, P).T)

    def conv_cols(l):
        taps = np.stack([*x["ffn_conv_w"][l], x["ffn_conv_b"][l]])
        return taps.reshape(4, 2 * FT, P).transpose(2, 1, 0).reshape(P, -1)

    cond = np.stack([x["c"][0], x["c_ctx"]]).reshape(2, KT, P).transpose(2, 1, 0).reshape(P, 16)
    dw = x["cm_dw_w"][0].reshape(CW, KT, P).transpose(2, 1, 0).reshape(P, KT * CW)
    vec = np.concatenate([cols(x["ada_b"][0]), cols(x["ada_b"][1]), cols(x["norm_g"]), cols(x["cm_b_in"][0]), dw,
                          cols(x["cm_dw_b"][0]), cols(x["cm_ln_g"][0]), cols(x["cm_ln_b"][0]), cols(x["cm_b_out"][0]), cond,
                          np.broadcast_to(x["attn_sink"][0][None, :], (P, NQ)), conv_cols(0), conv_cols(1)], axis=1)
    xT = np.concatenate([x["x"][0], x["ctx"][0]]).T.reshape(KT, P, TOK).transpose(1, 0, 2)
    consts, masks, rope = shape_constants()
    arrays = {"xT": xT, "wstream": wstream, "adastream": adastream, "vec": vec, "consts": consts,
              "bconsts": masks.astype(ml_dtypes.bfloat16), "rope": rope}
    arrays = {k: np.ascontiguousarray(v) for k, v in arrays.items()}
    nc = bacc.Bacc("TRN2", target_bir_lowering=False, num_devices=1)
    args = [nc.dram_tensor(k, v.shape, mybir.dt.from_np(v.dtype), kind="ExternalInput").ap() for k, v in arrays.items()]
    out = nc.dram_tensor("out", (P, KT, LAT), F32, kind="ExternalOutput").ap()
    backbone(nc, *args, out)
    r = run_bass_kernel_spmd(nc, [arrays], core_ids=[0])
    o = r.results[0]["out"]
    return np.ascontiguousarray(o.transpose(2, 1, 0).reshape(1, LAT, D))
```
